# Optimizing a Trainium2 kernel written in Bass

```python
import math
import jax, jax.numpy as jnp
from jax import lax
import numpy as np

D_MODEL = 1024
BATCH = 1
SEQ = 512
DEPTH = 2

HEAD_DIM = 64
GRID_W = 64
BLOCK = 128
NA_HEADS = 8
NA_ROW_K = 8
NA_COL_K = 16
SW_Q_HEADS = 8
SW_KV_HEADS = 2
SW_WINDOW = 128
DIFF_HEADS = 4
N_BRANCH = 3
BRANCH_W = 512
D_FF = 2816
ROPE_THETA = 10000.0
EPS = 1e-6
NEG = -1e30

A_W = NA_HEADS * HEAD_DIM
B_QW = SW_Q_HEADS * HEAD_DIM
B_KVW = SW_KV_HEADS * HEAD_DIM
C_QKW = 2 * DIFF_HEADS * HEAD_DIM
C_VW = DIFF_HEADS * 2 * HEAD_DIM
SPLIT_SIZES = (A_W, A_W, A_W, B_QW, B_KVW, B_KVW, C_QKW, C_QKW, C_VW, N_BRANCH * D_MODEL)
IN_COLS = sum(SPLIT_SIZES)


def rmsnorm(x, g):
    xf = x.astype(jnp.float32)
    y = xf * lax.rsqrt(jnp.mean(xf * xf, axis=-1, keepdims=True) + EPS)
    return (y * g.astype(jnp.float32)).astype(x.dtype)

def swiglu(x, w_gu, w_down):
    gate, up = jnp.split(x @ w_gu, 2, axis=-1)
    return (jax.nn.silu(gate) * up) @ w_down

def rope_tables(s):
    pos = jnp.arange(s, dtype=jnp.float32)
    inv = ROPE_THETA ** (-jnp.arange(0, HEAD_DIM, 2, dtype=jnp.float32) / HEAD_DIM)
    ang = pos[:, None] * inv[None, :]
    ang = jnp.concatenate([ang, ang], axis=-1)
    return jnp.cos(ang), jnp.sin(ang)

def apply_rope(t, cos, sin):
    t1, t2 = jnp.split(t, 2, axis=-1)
    rot = jnp.concatenate([-t2, t1], axis=-1)
    return t * cos.astype(t.dtype) + rot * sin.astype(t.dtype)

def split_heads(t, n):
    b, s, _ = t.shape
    return t.reshape(b, s, n, HEAD_DIM).transpose(0, 2, 1, 3)

def neighbourhood_attention(q, k, v, rpb):
    b, h, s, d = q.shape
    rows = s // GRID_W
    kr = min(NA_ROW_K, rows)
    kc = NA_COL_K
    r = jnp.arange(rows)
    c = jnp.arange(GRID_W)
    row_start = jnp.clip(r - kr // 2, 0, rows - kr)
    col_start = jnp.clip(c - kc // 2, 0, GRID_W - kc)
    key_rows = row_start[:, None] + jnp.arange(kr)[None, :]
    qg = q.reshape(b, h, rows, GRID_W, d)
    kg = k.reshape(b, h, rows, GRID_W, d)[:, :, key_rows]
    vg = v.reshape(b, h, rows, GRID_W, d)[:, :, key_rows]
    scores = jnp.einsum('bhrcd,bhrijd->bhrcij', qg, kg).astype(jnp.float32) * (d ** -0.5)
    dr = key_rows - r[:, None] + (NA_ROW_K - 1)
    dc = jnp.clip(c[None, :] - c[:, None] + (NA_COL_K - 1), 0, 2 * NA_COL_K - 2)
    bias = rpb[:, dr[:, None, :, None], dc[None, :, None, :]]
    col_ok = (c[None, :] >= col_start[:, None]) & (c[None, :] < col_start[:, None] + kc)
    scores = scores + bias[None].astype(jnp.float32)
    scores = jnp.where(col_ok[None, None, None, :, None, :], scores, NEG)
    p = jax.nn.softmax(scores.reshape(b, h, rows, GRID_W, kr * GRID_W), axis=-1)
    p = p.reshape(b, h, rows, GRID_W, kr, GRID_W).astype(v.dtype)
    out = jnp.einsum('bhrcij,bhrijd->bhrcd', p, vg)
    return out.reshape(b, h, s, d)

def sliding_window_attention(q, k, v, sink):
    b, hq, s, d = q.shape
    hkv = k.shape[1]
    g = hq // hkv
    nb = s // BLOCK
    qb = q.reshape(b, hkv, g, nb, BLOCK, d)

    def band(t):
        tp = jnp.pad(t, ((0, 0), (0, 0), (BLOCK, BLOCK), (0, 0))).reshape(b, hkv, nb + 2, BLOCK, d)
        return jnp.concatenate([tp[:, :, :-2], tp[:, :, 1:-1], tp[:, :, 2:]], axis=3)

    kb, vb = band(k), band(v)
    scores = jnp.einsum('bkgnqd,bknjd->bkgnqj', qb, kb).astype(jnp.float32) * (d ** -0.5)
    qpos = jnp.arange(nb)[:, None] * BLOCK + jnp.arange(BLOCK)[None, :]
    kpos = (jnp.arange(nb)[:, None] - 1) * BLOCK + jnp.arange(3 * BLOCK)[None, :]
    ok = ((jnp.abs(qpos[:, :, None] - kpos[:, None, :]) <= SW_WINDOW)
          & (kpos[:, None, :] >= 0) & (kpos[:, None, :] < s))
    scores = jnp.where(ok, scores, NEG)
    sink_logit = jnp.broadcast_to(sink.astype(jnp.float32).reshape(1, hkv, g, 1, 1, 1),
                                  scores.shape[:-1] + (1,))
    p = jax.nn.softmax(jnp.concatenate([scores, sink_logit], axis=-1), axis=-1)[..., :-1]
    out = jnp.einsum('bkgnqj,bknjd->bkgnqd', p.astype(v.dtype), vb)
    return out.reshape(b, hq, s, d)

def differential_attention(q, k, v, lam, lam_init, subln_g):
    b, h, _, s, d = q.shape
    nb = s // BLOCK
    qb = jnp.moveaxis(q.reshape(b, h, 2, nb, BLOCK, d), 3, 0)

    def one_block(qblk):
        sc = jnp.einsum('bhtqd,bhtkd->bhtqk', qblk, k).astype(jnp.float32) * (d ** -0.5)
        p = jax.nn.softmax(sc, axis=-1)
        a = p[:, :, 0] - lam * p[:, :, 1]
        return jnp.einsum('bhqk,bhke->bhqe', a.astype(v.dtype), v)

    o = lax.map(one_block, qb)
    o = jnp.moveaxis(o, 0, 2).reshape(b, h, s, 2 * d)
    return rmsnorm(o, subln_g) * (1.0 - lam_init)

def first_inputs(seed: int = 0) -> dict:
    key = jax.random.key(seed)
    ks = jax.random.split(key, 24)
    L, D, F = DEPTH, D_MODEL, D_FF

    def nrm(k, shape, scale):
        return jax.random.normal(k, shape, jnp.float32) * scale

    def gain(k, n):
        return 1.0 + nrm(k, (L, n), 0.05)

    return {
        "x": nrm(ks[0], (BATCH, SEQ, D), 1.0),
        "ffn1_pre_g": gain(ks[1], D),
        "ffn1_w_gu": nrm(ks[2], (L, D, 2 * F), D ** -0.5),
        "ffn1_w_down": nrm(ks[3], (L, F, D), F ** -0.5),
        "ffn1_post_g": gain(ks[4], D),
        "mix_pre_g": gain(ks[5], D),
        "w_in": nrm(ks[6], (L, D, IN_COLS), D ** -0.5),
        "na_rpb": nrm(ks[7], (L, NA_HEADS, 2 * NA_ROW_K - 1, 2 * NA_COL_K - 1), 0.5),
        "sw_sink": nrm(ks[8], (L, SW_Q_HEADS), 1.0),
        "diff_lambda_q1": nrm(ks[9], (L, HEAD_DIM), 0.1),
        "diff_lambda_k1": nrm(ks[10], (L, HEAD_DIM), 0.1),
        "diff_lambda_q2": nrm(ks[11], (L, HEAD_DIM), 0.1),
        "diff_lambda_k2": nrm(ks[12], (L, HEAD_DIM), 0.1),
        "diff_subln_g": gain(ks[13], 2 * HEAD_DIM),
        "w_branch": nrm(ks[14], (L, N_BRANCH, BRANCH_W, D), BRANCH_W ** -0.5),
        "b_gate": nrm(ks[15], (L, N_BRANCH, D), 0.1),
        "w_out": nrm(ks[16], (L, D, D), D ** -0.5),
        "mix_post_g": gain(ks[17], D),
        "ffn2_pre_g": gain(ks[18], D),
        "ffn2_w_gu": nrm(ks[19], (L, D, 2 * F), D ** -0.5),
        "ffn2_w_down": nrm(ks[20], (L, F, D), F ** -0.5),
        "ffn2_post_g": gain(ks[21], D),
    }

def first_block(x, ffn1_pre_g, ffn1_w_gu, ffn1_w_down, ffn1_post_g, mix_pre_g, w_in, na_rpb,
              sw_sink, diff_lambda_q1, diff_lambda_k1, diff_lambda_q2, diff_lambda_k2,
              diff_subln_g, w_branch, b_gate, w_out, mix_post_g, ffn2_pre_g, ffn2_w_gu,
              ffn2_w_down, ffn2_post_g):
    b, s, _ = x.shape
    cos, sin = rope_tables(s)
    split_at = np.cumsum(SPLIT_SIZES)[:-1].tolist()
    h = x
    for l in range(DEPTH):
        y = swiglu(rmsnorm(h, ffn1_pre_g[l]), ffn1_w_gu[l], ffn1_w_down[l])
        h = h + 0.5 * rmsnorm(y, ffn1_post_g[l])

        u = rmsnorm(h, mix_pre_g[l])
        proj = u @ w_in[l]
        qa, ka, va, qb, kb, vb, qc, kc, vc, gl = jnp.split(proj, split_at, axis=-1)

        oa = neighbourhood_attention(split_heads(qa, NA_HEADS), split_heads(ka, NA_HEADS),
                                     split_heads(va, NA_HEADS), na_rpb[l])
        oa = oa.transpose(0, 2, 1, 3).reshape(b, s, A_W)

        ob = sliding_window_attention(apply_rope(split_heads(qb, SW_Q_HEADS), cos, sin),
                                      apply_rope(split_heads(kb, SW_KV_HEADS), cos, sin),
                                      split_heads(vb, SW_KV_HEADS), sw_sink[l])
        ob = ob.transpose(0, 2, 1, 3).reshape(b, s, B_QW)

        qc = apply_rope(qc.reshape(b, s, DIFF_HEADS, 2, HEAD_DIM).transpose(0, 2, 3, 1, 4), cos, sin)
        kc = apply_rope(kc.reshape(b, s, DIFF_HEADS, 2, HEAD_DIM).transpose(0, 2, 3, 1, 4), cos, sin)
        vc = vc.reshape(b, s, DIFF_HEADS, 2 * HEAD_DIM).transpose(0, 2, 1, 3)
        lam_init = 0.8 - 0.6 * math.exp(-0.3 * l)
        lam = (jnp.exp(jnp.sum(diff_lambda_q1[l].astype(jnp.float32) * diff_lambda_k1[l].astype(jnp.float32)))
               - jnp.exp(jnp.sum(diff_lambda_q2[l].astype(jnp.float32) * diff_lambda_k2[l].astype(jnp.float32)))
               + lam_init)
        oc = differential_attention(qc, kc, vc, lam, lam_init, diff_subln_g[l])
        oc = oc.transpose(0, 2, 1, 3).reshape(b, s, C_VW)

        branches = jnp.stack([oa, ob, oc], axis=2)
        yb = jnp.einsum('bsnc,ncd->bsnd', branches, w_branch[l])
        gates = jax.nn.sigmoid(gl.reshape(b, s, N_BRANCH, D_MODEL) + b_gate[l])
        merged = jnp.sum(gates * yb, axis=2)
        h = h + rmsnorm(merged @ w_out[l], mix_post_g[l])

        y = swiglu(rmsnorm(h, ffn2_pre_g[l]), ffn2_w_gu[l], ffn2_w_down[l])
        h = h + 0.5 * rmsnorm(y, ffn2_post_g[l])
    return h


DEPTH_2 = 1

N_META = 16
NEG_INF = -1e30
SWA_WINDOW = 128
SWA_Q_HEADS = 8
SWA_KV_HEADS = 2
SWA_GROUP = SWA_Q_HEADS // SWA_KV_HEADS
FOX_HEADS = 8
LRU_WIDTH = D_MODEL // 2
LRU_BLOCKS = 8
LRU_BLOCK_DIM = LRU_WIDTH // LRU_BLOCKS
CONV_WIDTH = 4
LRU_C = 8.0
REL_BUCKETS = 32
REL_MAX_DIST = 128
D_FF_2 = ((-(-8 * D_MODEL // 3)) + 255) // 256 * 256
SPLIT_SIZES_2 = (
    SWA_Q_HEADS * HEAD_DIM,
    SWA_KV_HEADS * HEAD_DIM,
    SWA_KV_HEADS * HEAD_DIM,
    FOX_HEADS * HEAD_DIM,
    FOX_HEADS * HEAD_DIM,
    FOX_HEADS * HEAD_DIM,
    FOX_HEADS,
    LRU_WIDTH,
    LRU_WIDTH,
    N_BRANCH * D_MODEL,
)
IN_COLS_2 = sum(SPLIT_SIZES_2)


def rms_norm(x, g, eps=1e-6):
    xf = x.astype(jnp.float32)
    y = xf * lax.rsqrt(jnp.mean(xf * xf, axis=-1, keepdims=True) + eps)
    return (y * g.astype(jnp.float32)).astype(x.dtype)

def pad_left(a, n):
    return jnp.pad(a, [(0, 0), (n, 0)] + [(0, 0)] * (a.ndim - 2))

def t5_bucket(dist):
    max_exact = REL_BUCKETS // 2
    d = jnp.maximum(dist, 0)
    scaled = jnp.log(jnp.maximum(d, 1).astype(jnp.float32) / max_exact) / math.log(REL_MAX_DIST / max_exact)
    large = jnp.minimum(max_exact + (scaled * (REL_BUCKETS - max_exact)).astype(jnp.int32), REL_BUCKETS - 1)
    return jnp.where(d < max_exact, d, large)

def swa_sink_attention(q, k, v, sinks, rel_table, n_pad):
    b, tp, _, dh = q.shape
    nb = tp // BLOCK
    qb = q.reshape(b, nb, BLOCK, SWA_KV_HEADS, SWA_GROUP, dh)

    def band(a):
        a = a.reshape(b, nb, BLOCK, SWA_KV_HEADS, dh)
        prev = jnp.pad(a, ((0, 0), (1, 0), (0, 0), (0, 0), (0, 0)))[:, :-1]
        return jnp.concatenate([prev, a], axis=2)

    k_band, v_band = band(k), band(v)
    s = jnp.einsum('bnqhgd,bnkhd->bnhgqk', qb, k_band).astype(jnp.float32) * (dh ** -0.5)
    q_idx = jnp.arange(BLOCK)[:, None]
    k_idx = jnp.arange(2 * BLOCK)[None, :]
    dist = q_idx + BLOCK - k_idx
    bias = rel_table.astype(jnp.float32)[t5_bucket(dist)]
    bias = bias.transpose(2, 0, 1).reshape(SWA_KV_HEADS, SWA_GROUP, BLOCK, 2 * BLOCK)
    key_abs = (jnp.arange(nb)[:, None] - 1) * BLOCK + k_idx
    mask = ((dist >= 0) & (dist < SWA_WINDOW))[None] & (key_abs >= n_pad)[:, None, :]
    s = jnp.where(mask[None, :, None, None], s + bias, NEG_INF)
    sink = sinks.astype(jnp.float32).reshape(SWA_KV_HEADS, SWA_GROUP)[None, None, :, :, None, None]
    m = jnp.maximum(jnp.max(s, axis=-1, keepdims=True), sink)
    p = jnp.exp(s - m)
    denom = jnp.sum(p, axis=-1, keepdims=True) + jnp.exp(sink - m)
    p = (p / denom).astype(v.dtype)
    o = jnp.einsum('bnhgqk,bnkhd->bnqhgd', p, v_band)
    return o.reshape(b, tp, SWA_Q_HEADS * dh)

def forgetting_attention(q, k, v, log_f, n_pad):
    b, tp, h, dh = q.shape
    nb = tp // BLOCK
    cum = jnp.cumsum(log_f, axis=1).transpose(0, 2, 1)
    k_pos = jnp.arange(tp)
    qb = q.reshape(b, nb, BLOCK, h, dh).transpose(1, 0, 2, 3, 4)
    cb = cum.reshape(b, h, nb, BLOCK).transpose(2, 0, 1, 3)

    def one_block(args):
        qi, ci, n = args
        s = jnp.einsum('bqhd,bkhd->bhqk', qi, k).astype(jnp.float32) * (dh ** -0.5)
        s = s + ci[..., :, None] - cum[:, :, None, :]
        q_pos = n * BLOCK + jnp.arange(BLOCK)
        mask = (k_pos[None, :] <= q_pos[:, None]) & (k_pos >= n_pad)[None, :]
        s = jnp.where(mask, s, NEG_INF)
        p = jax.nn.softmax(s, axis=-1).astype(v.dtype)
        return jnp.einsum('bhqk,bkhd->bqhd', p, v)

    o = lax.map(one_block, (qb, cb, jnp.arange(nb)))
    return o.transpose(1, 0, 2, 3, 4).reshape(b, tp, h * dh)

def causal_depthwise_conv(x, w, bias):
    t = x.shape[1]
    xp = jnp.pad(x, ((0, 0), (CONV_WIDTH - 1, 0), (0, 0)))
    out = xp[:, 0:t] * w[0]
    for i in range(1, CONV_WIDTH):
        out = out + xp[:, i:i + t] * w[i]
    return out + bias

def rg_lru(x, w_r, b_r, w_i, b_i, lam):
    b, t, c = x.shape
    xb = x.reshape(b, t, LRU_BLOCKS, LRU_BLOCK_DIM)
    r = jax.nn.sigmoid(jnp.einsum('bthi,hij->bthj', xb, w_r).reshape(b, t, c).astype(jnp.float32) + b_r)
    gi = jax.nn.sigmoid(jnp.einsum('bthi,hij->bthj', xb, w_i).reshape(b, t, c).astype(jnp.float32) + b_i)
    log_a = LRU_C * r * jax.nn.log_sigmoid(lam.astype(jnp.float32))
    a = jnp.exp(log_a)
    inp = jnp.sqrt(-jnp.expm1(2.0 * log_a)) * (gi * x.astype(jnp.float32))

    def combine(left, right):
        a1, b1 = left
        a2, b2 = right
        return a1 * a2, a2 * b1 + b2

    _, h = lax.associative_scan(combine, (a, inp), axis=1)
    return h.astype(x.dtype)

def second_inputs(seed: int = 0) -> dict:
    key = jax.random.key(seed)
    ks = jax.random.split(key, 24)
    f32 = jnp.float32
    nrm = lambda k, shape, scale: jax.random.normal(k, shape, f32) * scale
    u = jax.random.uniform(ks[10], (DEPTH_2, LRU_WIDTH), f32, 0.9, 0.999)
    a0 = u ** (1.0 / LRU_C)
    return {
        "x": nrm(ks[0], (BATCH, SEQ, D_MODEL), 1.0),
        "meta_tokens": nrm(ks[1], (N_META, D_MODEL), 1.0),
        "rel_bias_table": nrm(ks[2], (REL_BUCKETS, SWA_Q_HEADS), 0.5),
        "norm_mix": 1.0 + nrm(ks[3], (DEPTH_2, D_MODEL), 0.02),
        "w_in": nrm(ks[4], (DEPTH_2, D_MODEL, IN_COLS_2), D_MODEL ** -0.5),
        "swa_sinks": nrm(ks[5], (DEPTH_2, SWA_Q_HEADS), 0.5),
        "fox_forget_bias": 2.0 + 3.0 * jax.random.uniform(ks[6], (DEPTH_2, FOX_HEADS), f32),
        "conv_w": nrm(ks[7], (DEPTH_2, CONV_WIDTH, LRU_WIDTH), CONV_WIDTH ** -0.5),
        "conv_b": nrm(ks[8], (DEPTH_2, LRU_WIDTH), 0.02),
        "lru_w_r": nrm(ks[9], (DEPTH_2, LRU_BLOCKS, LRU_BLOCK_DIM, LRU_BLOCK_DIM), LRU_BLOCK_DIM ** -0.5),
        "lru_b_r": nrm(ks[11], (DEPTH_2, LRU_WIDTH), 0.02),
        "lru_w_i": nrm(ks[12], (DEPTH_2, LRU_BLOCKS, LRU_BLOCK_DIM, LRU_BLOCK_DIM), LRU_BLOCK_DIM ** -0.5),
        "lru_b_i": nrm(ks[13], (DEPTH_2, LRU_WIDTH), 0.02),
        "lru_lambda": jnp.log(a0) - jnp.log1p(-a0),
        "w_branch": nrm(ks[14], (DEPTH_2, N_BRANCH, LRU_WIDTH, D_MODEL), LRU_WIDTH ** -0.5),
        "w_out": nrm(ks[15], (DEPTH_2, D_MODEL, D_MODEL), D_MODEL ** -0.5),
        "norm_ffn": 1.0 + nrm(ks[16], (DEPTH_2, D_MODEL), 0.02),
        "w_ffn_in": nrm(ks[17], (DEPTH_2, D_MODEL, 2 * D_FF_2), D_MODEL ** -0.5),
        "w_ffn_out": nrm(ks[18], (DEPTH_2, D_FF_2, D_MODEL), D_FF_2 ** -0.5),
        "norm_final": 1.0 + nrm(ks[19], (D_MODEL,), 0.02),
    }

def second_block(x, meta_tokens, rel_bias_table, norm_mix, w_in, swa_sinks, fox_forget_bias, conv_w, conv_b,
              lru_w_r, lru_b_r, lru_w_i, lru_b_i, lru_lambda, w_branch, w_out, norm_ffn, w_ffn_in,
              w_ffn_out, norm_final):
    b = x.shape[0]
    meta = jnp.broadcast_to(meta_tokens.astype(x.dtype)[None], (b, N_META, D_MODEL))
    h = jnp.concatenate([meta, x], axis=1)
    t = h.shape[1]
    n_pad = (-t) % BLOCK
    split_points = [int(p) for p in np.cumsum(SPLIT_SIZES_2)[:-1]]
    for l in range(DEPTH_2):
        u = rms_norm(h, norm_mix[l])
        proj = u @ w_in[l]
        qa, ka, va, qf, kf, vf, fl, xc, yc, gates = jnp.split(proj, split_points, axis=-1)
        o_a = swa_sink_attention(
            pad_left(qa.reshape(b, t, SWA_Q_HEADS, HEAD_DIM), n_pad),
            pad_left(ka.reshape(b, t, SWA_KV_HEADS, HEAD_DIM), n_pad),
            pad_left(va.reshape(b, t, SWA_KV_HEADS, HEAD_DIM), n_pad),
            swa_sinks[l], rel_bias_table, n_pad)[:, n_pad:]
        log_f = jax.nn.log_sigmoid(fl.astype(jnp.float32) + fox_forget_bias[l].astype(jnp.float32))
        o_f = forgetting_attention(
            pad_left(qf.reshape(b, t, FOX_HEADS, HEAD_DIM), n_pad),
            pad_left(kf.reshape(b, t, FOX_HEADS, HEAD_DIM), n_pad),
            pad_left(vf.reshape(b, t, FOX_HEADS, HEAD_DIM), n_pad),
            pad_left(log_f, n_pad), n_pad)[:, n_pad:]
        xc = causal_depthwise_conv(xc, conv_w[l], conv_b[l])
        o_c = rg_lru(xc, lru_w_r[l], lru_b_r[l], lru_w_i[l], lru_b_i[l], lru_lambda[l]) * jax.nn.gelu(yc)
        g = jax.nn.sigmoid(gates).reshape(b, t, N_BRANCH, D_MODEL)
        merged = (g[:, :, 0] * (o_a @ w_branch[l, 0])
                  + g[:, :, 1] * (o_f @ w_branch[l, 1])
                  + g[:, :, 2] * (o_c @ w_branch[l, 2]))
        h = h + merged @ w_out[l]
        u = rms_norm(h, norm_ffn[l])
        gate_ff, up_ff = jnp.split(u @ w_ffn_in[l], 2, axis=-1)
        h = h + (jax.nn.silu(gate_ff) * up_ff) @ w_ffn_out[l]
    return rms_norm(h, norm_final)[:, N_META:]


def setup_inputs(seed=0):
    out = dict(first_inputs(seed))
    for name, value in second_inputs(seed + 1).items():
        if name != "x":
            out[name + "_2"] = value
    return out


def reference(
    x, ffn1_pre_g, ffn1_w_gu, ffn1_w_down, ffn1_post_g, mix_pre_g, w_in, na_rpb, sw_sink,
    diff_lambda_q1, diff_lambda_k1, diff_lambda_q2, diff_lambda_k2, diff_subln_g, w_branch,
    b_gate, w_out, mix_post_g, ffn2_pre_g, ffn2_w_gu, ffn2_w_down, ffn2_post_g, meta_tokens_2,
    rel_bias_table_2, norm_mix_2, w_in_2, swa_sinks_2, fox_forget_bias_2, conv_w_2, conv_b_2,
    lru_w_r_2, lru_b_r_2, lru_w_i_2, lru_b_i_2, lru_lambda_2, w_branch_2, w_out_2, norm_ffn_2,
    w_ffn_in_2, w_ffn_out_2, norm_final_2,
):
    x = first_block(
        x, ffn1_pre_g, ffn1_w_gu, ffn1_w_down, ffn1_post_g, mix_pre_g, w_in, na_rpb, sw_sink,
        diff_lambda_q1, diff_lambda_k1, diff_lambda_q2, diff_lambda_k2, diff_subln_g, w_branch,
        b_gate, w_out, mix_post_g, ffn2_pre_g, ffn2_w_gu, ffn2_w_down, ffn2_post_g,
    )
    return second_block(
        x, meta_tokens_2, rel_bias_table_2, norm_mix_2, w_in_2, swa_sinks_2, fox_forget_bias_2,
        conv_w_2, conv_b_2, lru_w_r_2, lru_b_r_2, lru_w_i_2, lru_b_i_2, lru_lambda_2,
        w_branch_2, w_out_2, norm_ffn_2, w_ffn_in_2, w_ffn_out_2, norm_final_2,
    )


_drawn_inputs = setup_inputs


def setup_inputs(seed=0):
    import zlib

    import numpy as np

    out = dict(_drawn_inputs(seed))
    spreads = {}
    factors = {'sw_sink': 8.0,
     'rel_bias_table_2': 3.363,
     'norm_mix_2': 4.657,
     'swa_sinks_2': 200.0,
     'conv_b_2': 3.486,
     'lru_b_r_2': 32.579,
     'lru_b_i_2': 8.0,
     'norm_ffn_2': 7.299}
    for name, (base, spread) in spreads.items():
        noise = np.random.default_rng([zlib.crc32(name.encode()), seed]).standard_normal(out[name].shape)
        drawn = base * np.exp(spread * noise) if base else spread * noise
        out[name] = __import__('jax').numpy.asarray(drawn.astype(out[name].dtype))
    for name, factor in factors.items():
        out[name] = (out[name] * factor).astype(out[name].dtype)
    return out
```

```python
import math
from contextlib import ExitStack

import numpy as np

import concourse.bass as bass
from concourse import mybir

F32 = mybir.dt.float32
F32R = mybir.dt.float32r
ALU = mybir.AluOpType
ACT = mybir.ActivationFunctionType
AX = mybir.AxisListType

P = 128
D = 1024
KT = 8
FT = 22
TW = 528
X0 = 16
NEG = -1e30
LOWEST = -3.0e38

PCOLS = {}
_n = 0
for _l in range(2):
    for _name, _w in (("f1pre", 8), ("f1post", 8), ("mpre", 8), ("mpost", 8), ("f2pre", 8), ("f2post", 8),
                      ("sink", 8), ("subg", 1), ("bgate", 24)):
        PCOLS[_name, _l] = _n
        _n += _w
for _name, _w in (("mpre", 8), ("fpre", 8), ("final", 8), ("sink", 8), ("foxb", 1), ("convw", 16), ("convb", 4),
                  ("br", 4), ("bi", 4), ("lam", 4)):
    PCOLS[_name, 2] = _n
    _n += _w
NPAR = _n


class Engine:

    def __init__(self, sem, always, serial=False):
        self.sem, self.always, self.serial = sem, always, serial
        self.queue, self.count, self.waited = [], 0, {}

    def __call__(self, make, *after, inc=False):
        waits = []
        if self.serial and self.count:
            after = (after, (self.sem, self.count))
        for sem, value in flat(after):
            if self.waited.get(id(sem), 0) < value:
                self.waited[id(sem)] = value
                waits.append((sem, value))
        inc = inc or self.always
        self.queue.append((waits, make, (self.sem, 1) if inc else None))
        if inc:
            self.count += 1
            return (self.sem, self.count)
        return None

    def dma(self, slot, make, *after):
        self(make, *after)
        if self.always:
            self.count -= 1
        waits, fn, _ = self.queue[-1]
        self.queue[-1] = (waits, fn, (slot.sem, 16))
        slot.count += 16
        return (slot.sem, slot.count)


class Slot:
    def __init__(self, sem):
        self.sem, self.count = sem, 0


class Buf:

    def __init__(self, ap):
        self.ap, self.free, self.taken = ap, [], 0


class Ring:
    def __init__(self, bufs):
        self.bufs, self.n = bufs, 0

    def take(self):
        b = min((b for b in self.bufs if b.free is not None), key=lambda b: b.taken)
        self.n += 1
        b.taken, b.old, b.free = self.n, b.free, None
        return b


def flat(x):
    for y in x:
        if y is None:
            continue
        if isinstance(y, tuple) and len(y) == 2 and isinstance(y[1], int):
            yield y
        else:
            yield from flat(y)


def consts():
    f = np.float32
    c = {}
    c["ident"] = np.eye(P, dtype=f)
    c["ones"] = np.ones((P, P), f)
    pos = np.arange(512, dtype=f)
    inv = (f(10000.0) ** (-np.arange(0, 64, 2, dtype=f) / f(64))).astype(f)
    ang = (pos[:, None] * inv[None, :]).astype(f)
    cos, sin = np.cos(ang).astype(f).T, np.sin(ang).astype(f).T
    c["cos"] = np.concatenate([cos] * 4, 0)
    c["sin"] = np.concatenate([sin, -sin] * 2, 0)
    col = np.arange(64)
    start = np.clip(col - 8, 0, 48)
    ok = (col[None, :] >= start[:, None]) & (col[None, :] < start[:, None] + 16)
    m = np.where(ok, 0.0, NEG).astype(f)
    c["mask_a"] = np.concatenate([m, m], 0)
    q, k = np.arange(P)[:, None], np.arange(3 * P)[None, :]
    c["mask_b"] = np.where(np.abs(q + P - k) <= 128, 0.0, NEG).astype(f)
    k2 = np.arange(2 * P)[None, :]
    dist = q + P - k2
    c["mask_s"] = np.where((dist >= 0) & (dist < 128), 0.0, NEG).astype(f)
    k1 = np.arange(P)[None, :]
    c["mask_t"] = np.where(k1 <= q, 0.0, NEG).astype(f)
    d = np.arange(128)
    scaled = np.log(np.maximum(d, 1).astype(f) / f(16)) / f(math.log(128 / 16))
    large = np.minimum(16 + (scaled * 16).astype(np.int32), 31)
    bucket = np.where(d < 16, d, large)
    oh = np.zeros((32, 384), f)
    oh[bucket, 255 - d] = 1.0
    c["onehot"] = oh
    return c


def tiles_t(w):
    k, n = w.shape
    return np.ascontiguousarray(w.reshape(k // P, P, n // P, P).transpose(2, 1, 0, 3))


def tiles_v(w):
    k, n = w.shape
    return np.ascontiguousarray(w.reshape(k // 256, 2, P, n).transpose(0, 2, 1, 3))


PAIRED = np.concatenate([np.arange(64) + 64 * h for t in range(4) for h in (t, t + 4)])


def pack(x):
    f = np.float32
    out = {}
    out["xt"] = np.ascontiguousarray(x["x"][0].T.reshape(KT, P, 512))
    out["metat"] = np.ascontiguousarray(x["meta_tokens_2"].T.reshape(KT, P, 16))
    out["gu"] = np.stack([tiles_t(a) for a in (x["ffn1_w_gu"][0], x["ffn2_w_gu"][0], x["ffn1_w_gu"][1],
                                               x["ffn2_w_gu"][1], x["w_ffn_in_2"][0])])
    out["dn"] = np.stack([tiles_t(a) for a in (x["ffn1_w_down"][0], x["ffn2_w_down"][0], x["ffn1_w_down"][1],
                                               x["ffn2_w_down"][1], x["w_ffn_out_2"][0])])
    ins, vs, brs = [], [], []
    for l in range(2):
        w = x["w_in"][l]
        ins.append(tiles_t(np.concatenate([w[:, 0:1024], w[:, 1536:2048][:, PAIRED], w[:, 2048:2304],
                                           w[:, 2304:3328], w[:, 3840:6912]], 1)))
        vs.append(np.stack([tiles_v(w[:, 1024:1536]), tiles_v(w[:, 3328:3840])]))
        b = x["w_branch"][l]
        brs.append(np.stack([tiles_t(b[0]), tiles_t(b[1][PAIRED]), tiles_t(b[2])]))
    out["win"], out["wv"] = np.stack(ins), np.stack(vs)
    w = x["w_in_2"][0]
    fl = np.concatenate([w[:, 2304:2312], np.zeros((D, 120), f)], 1)
    out["win2"] = tiles_t(np.concatenate([w[:, 0:512][:, PAIRED], w[:, 512:768], w[:, 768:1792], fl,
                                          w[:, 2312:3336], w[:, 3336:6408]], 1))
    out["wv2"] = tiles_v(w[:, 1792:2304])
    b = x["w_branch_2"][0]
    brs.append(np.stack([tiles_t(b[0][PAIRED]), tiles_t(b[1]), tiles_t(b[2])]))
    out["wbr"] = np.stack(brs)
    out["wout"] = np.stack([tiles_t(x["w_out"][0]), tiles_t(x["w_out"][1]), tiles_t(x["w_out_2"][0])])
    par = np.zeros((P, NPAR), f)

    def put(name, l, a):
        par[:, PCOLS[name, l]:PCOLS[name, l] + a.shape[1]] = a

    def cols(v):
        return v.reshape(-1, P).T

    for l in range(2):
        for name, src in (("f1pre", "ffn1_pre_g"), ("f1post", "ffn1_post_g"), ("mpre", "mix_pre_g"),
                          ("mpost", "mix_post_g"), ("f2pre", "ffn2_pre_g"), ("f2post", "ffn2_post_g"),
                          ("subg", "diff_subln_g")):
            put(name, l, cols(x[src][l]))
        put("sink", l, np.broadcast_to(x["sw_sink"][l], (P, 8)))
        put("bgate", l, cols(x["b_gate"][l].reshape(-1)))
    put("mpre", 2, cols(x["norm_mix_2"][0]))
    put("fpre", 2, cols(x["norm_ffn_2"][0]))
    put("final", 2, cols(x["norm_final_2"]))
    put("sink", 2, np.broadcast_to(x["swa_sinks_2"][0], (P, 8)))
    par[0:8, PCOLS["foxb", 2]] = x["fox_forget_bias_2"][0]
    put("convw", 2, cols(x["conv_w_2"][0].reshape(-1)))
    put("convb", 2, cols(x["conv_b_2"][0]))
    put("br", 2, cols(x["lru_b_r_2"][0]))
    put("bi", 2, cols(x["lru_b_i_2"][0]))
    put("lam", 2, cols(x["lru_lambda_2"][0]))
    out["par"] = par
    out["lamv"] = np.ascontiguousarray(np.broadcast_to(np.stack(
        [np.concatenate([x[f"diff_lambda_{a}"][l] for a in ("q1", "k1", "q2", "k2")]) for l in range(2)]
    ).reshape(1, 512), (P, 512)))
    rp = np.zeros((2, 8, 15, 64, P), f)
    rp[..., 48:79] = x["na_rpb"][:, :, :, None, :]
    out["rpb"] = rp
    lw = np.zeros((2, 4, P, P), f)
    for i, name in enumerate(("lru_w_r_2", "lru_w_i_2")):
        for b in range(8):
            o = 64 * (b % 2)
            lw[i, b // 2, o:o + 64, o:o + 64] = x[name][0][b]
    out["lruw"] = np.ascontiguousarray(lw.transpose(2, 0, 1, 3)).reshape(P, 1024)
    out["rel"] = np.ascontiguousarray(x["rel_bias_table_2"])
    for k, v in consts().items():
        out["c_" + k] = np.ascontiguousarray(v)
    return out


def build(nc, T, OUT, CUM, RELV, limit=99):
    ctx = ExitStack()
    with ctx:
        def sem(name):
            return ctx.enter_context(nc.semaphore(name))

        at = [16512]
        where = {}

        def area(name, size):
            where[name] = at[0]
            at[0] += size

        def sb(name, shape, dt, offset):
            return nc.alloc_sbuf_tensor_at(name, list(shape), dt, offset=offset)

        for name, size in (("h", 8 * TW * 4), ("uh", 8 * TW * 4), ("ul", 8 * TW * 4), ("raw", 3 * 4096),
                           ("split", 4 * 8192), ("tmp", 6 * TW * 4), ("acc", TW * 4), ("rb", 2 * TW * 4),
                           ("small", 1024), ("par", 1280), ("ident", 512), ("ones", 512), ("maskt", 512),
                           ("X", 44 * TW * 4)):
            area(name, size)
        h = sb("h", [P, 8, TW], F32, where["h"])
        uh = sb("uh", [P, 8, TW], F32R, where["uh"])
        ul = sb("ul", [P, 8, TW], F32R, where["ul"])
        y_u = sb("y_u", [P, 8, TW], F32, where["uh"])
        raw = sb("raw", [P, 3, 1024], F32, where["raw"])
        wh = sb("wh", [P, 4, 1024], F32R, where["split"])
        wl = sb("wl", [P, 4, 1024], F32R, where["split"] + 4 * 4096)
        tmpt = sb("tmpt", [P, 6, TW], F32, where["tmp"])
        acc = sb("acc", [P, TW], F32, where["acc"])
        rb = sb("rb", [P, 2, TW], F32, where["rb"])
        small = sb("small", [P, 256], F32, where["small"])
        par = sb("par", [P, NPAR + 64], F32, where["par"])
        ident = sb("ident", [P, P], F32, where["ident"])
        ones = sb("ones", [P, P], F32, where["ones"])
        maskt = sb("maskt", [P, P], F32, where["maskt"])
        X = where["X"]
        gh = sb("gh", [P, FT, TW], F32R, X)
        gl = sb("gl", [P, FT, TW], F32R, X + FT * TW * 4)
        stk = sb("stk", [P, 12, TW], F32R, X)
        y_x = sb("y_x", [P, 8, TW], F32, X)
        lru = sb("lru", [P, 20, 532], F32, X)
        XV = X + 12 * TW * 4
        V = sb("V", [P, 5, 512], F32, XV)
        PT = sb("PT", [P, 5, 512], F32, XV + 10240)
        XG = XV + 20480
        gates = sb("gates", [P, 2, TW], F32, XG)
        macc = sb("macc", [P, 8, TW], F32, XG + 2 * TW * 4)
        obh = sb("obh", [P, 4, TW], F32R, XG + 10 * TW * 4)
        obf = sb("obf", [P, 4, TW], F32, XG + 10 * TW * 4)
        obl = sb("obl", [P, 4, TW], F32R, XG + 14 * TW * 4)
        XT = XG + 18 * TW * 4
        tb = sb("tb", [P, 2, 896], F32, XT)
        maska = sb("maska", [P, 64], F32, XT + 7168)
        cos = sb("cos", [P, 512], F32, XT)
        sin = sb("sin", [P, 512], F32, XT + 2048)
        maskb = sb("maskb", [P, 384], F32, XT + 4096)
        sbias = sb("sbias", [P, 2, 256], F32, XT)
        masks = sb("masks", [P, 256], F32, XT + 2048)
        onehot = sb("onehot", [32, 384], F32, XT + 3072)
        relt = sb("relt", [32, 8], F32, XT + 4608)
        relv = sb("relv", [8, 384], F32, XT + 4640)
        cumb = sb("cumb", [P, 2, TW], F32, XT)
        ci = sb("ci", [P, 5, 8], F32, XT + 4224)
        cumt = sb("cumt", [8, TW], F32, XT + 4384)
        ptm = sb("ptm", [16, 16], F32, XT + 6496)
        assert NPAR * 4 + 256 <= 1280 and XT + 7168 + 256 <= X + 44 * TW * 4 <= nc.sbuf_usable_end

        PS = ctx.enter_context(nc.psum_tensor("PS", [P, 4096], F32))
        banks = [Buf(PS[:, 512 * i:512 * i + 512]) for i in range(8)]

        pe = Engine(sem("s_pe"), False)
        act = Engine(sem("s_act"), True)
        dve = Engine(sem("s_dve"), True)
        pool = Engine(sem("s_pool"), True, True)
        sp = Engine(None, False)
        raw_slots = [Slot(sem(f"s_raw{i}")) for i in range(3)]
        s_ld = {}

        def slot(name):
            if name not in s_ld:
                s_ld[name] = Slot(sem("s_" + name))
            return s_ld[name]

        def mm(out, lhsT, rhs, start, stop):
            return lambda e: e.matmul(out, lhsT, rhs, start=start, stop=stop, skip_group_check=True)

        def tr(out, in_, idn):
            return lambda e: e.transpose(out, in_, idn)

        def fn(out, in_, f, bias=None, scale=1.0, accum=None):
            kw = {} if bias is None else {"bias": bias}
            if accum is not None:
                kw["accum_out"] = accum
            return lambda e: e.activation(out, in_, f, scale=scale, **kw)

        def tt(out, a, b, op):
            return lambda e: e.tensor_tensor(out, a, b, op)

        def ts(out, a, s1, s2, op0, op1=None):
            if op1 is None:
                return lambda e: e.tensor_scalar(out, a, s1, None, op0)
            return lambda e: e.tensor_scalar(out, a, s1, s2, op0, op1)

        def stt(out, a, s, b, op0, op1):
            return lambda e: e.scalar_tensor_tensor(out, a, s, b, op0, op1)

        def rcp(out, a):
            return lambda e: e.reciprocal(out, a)

        def cp(out, a):
            return lambda e: e.tensor_copy(out, a)

        def ld(out, in_):
            return lambda e: e.dma_start(out, in_)

        MUL, ADD, SUB, MAX, MIN = ALU.mult, ALU.add, ALU.subtract, ALU.max, ALU.min

        def pcol(name, l, i=0):
            c = PCOLS[name, l] + i
            return par[:, c:c + 1]

        HB = NPAR
        EPSC, NLAM, SUBG, C8 = NPAR + 48, NPAR + 49, NPAR + 51, NPAR + 53
        NC8 = NPAR + 57
        eps = par[:, EPSC:EPSC + 1]

        t_par = sp.dma(slot("par"), ld(par[:, 0:NPAR], T["par"]))
        t_id = sp.dma(slot("id"), ld(ident[:, :], T["c_ident"]))
        t_on = sp.dma(slot("on"), ld(ones[:, :], T["c_ones"]))
        t_x = []
        for m in range(KT):
            t_x.append(sp.dma(slot(f"x{m}"), ld(h[:, m, X0:TW], T["xt"][m])))
        temps = Ring([Buf(tmpt[:, i, :]) for i in range(6)])
        b = temps.take()
        t_lv = sp.dma(slot("lv"), ld(b.ap[:, 0:512], T["lamv"]), b.old)
        t_mt = sp.dma(slot("mt"), ld(maskt[:, :], T["c_mask_t"]))
        t_eps = dve(lambda e: e.memset(eps, 1e-6))
        t_hb = []
        for l in range(2):
            c = PCOLS["bgate", l]
            t_hb.append(dve(ts(par[:, HB + 24 * l:HB + 24 * l + 24], par[:, c:c + 24], 0.5, None, MUL), t_par))
            lam_init = 0.8 - 0.6 * math.exp(-0.3 * l)
            t_sg = dve(ts(par[:, SUBG + l:SUBG + l + 1], pcol("subg", l), 1.0 - lam_init, None, MUL), t_par)
            t_hb.append(t_sg)
        b2 = temps.take()
        lv = b.ap[:, 0:512].rearrange("p (l a k d) -> p l a k d", l=2, a=2, k=2)
        pr = b2.ap[:, 0:256].rearrange("p (l a d) -> p l a d", l=2, a=2)
        t1 = None
        for l in range(2):
            t1 = dve(tt(pr[:, l, :, :], lv[:, l, :, 0, :], lv[:, l, :, 1, :], MUL), t_lv, b2.old)
        t2 = dve(lambda e: e.tensor_reduce(small[:, 0:4].rearrange("p (l a) -> p l a", l=2), pr, AX.X, ADD), t1)
        t3 = act(fn(small[:, 4:8], small[:, 0:4], ACT.Exp), t2)
        sv = small[:, 4:8].rearrange("p (l a) -> p l a", l=2)
        t4 = dve(tt(par[:, NLAM:NLAM + 2], sv[:, :, 1], sv[:, :, 0], SUB), t3)
        for l in range(2):
            lam_init = 0.8 - 0.6 * math.exp(-0.3 * l)
            c = par[:, NLAM + l:NLAM + l + 1]
            t_lam = dve(ts(c, c, -lam_init, None, ADD), t4)
        b.free, b2.free = [t1], [t2]
        t_lamall = t_lam

        class Weights:

            def __init__(self, order):
                self.order, self.asked = order, []
                self.loaded, self.cut = {}, {}
                self.n_load = self.n_cut = 0
                self.raw_free = [None] * 3
                self.cut_free = [[] for _ in range(4)]

            def load(self):
                i = self.n_load
                if i >= len(self.order):
                    return
                name, idx, k0, kn = self.order[i]
                src = T[name][idx]
                n = kn * P
                if name in ("wv", "wv2"):
                    src = src.rearrange("p k n -> p (k n)")
                    n = 1024
                else:
                    src = src[:, k0:k0 + kn, :].rearrange("p k n -> p (k n)")
                self.loaded[i] = (sp.dma(raw_slots[i % 3], ld(raw[:, i % 3, 0:n], src), self.raw_free[i % 3]), n)
                self.n_load += 1

            def split(self):
                i = self.n_cut
                if i >= len(self.order):
                    return
                while self.n_load <= i:
                    self.load()
                t, n = self.loaded[i]
                r, a, b_ = raw[:, i % 3, 0:n], wh[:, i % 4, 0:n], wl[:, i % 4, 0:n]
                t_h = act(fn(a, r, ACT.Copy), t, self.cut_free[i % 4])
                t_l = dve(tt(b_, r, a, SUB), t_h, self.cut_free[i % 4])
                self.cut[i] = (t_h, t_l)
                self.raw_free[i % 3] = [t_h, t_l]
                self.n_cut += 1
                while self.n_load < i + 4 and self.n_load < len(self.order):
                    self.load()

            def get(self, spec):
                i = len(self.asked)
                self.asked.append(spec)
                if self.order and self.order is not self.asked:
                    assert self.order[i] == spec
                    while self.n_cut <= i:
                        self.split()
                    toks = self.cut[i]
                else:
                    toks = None
                return i, wh[:, i % 4, :], wl[:, i % 4, :], toks

            def done(self, i, tok):
                self.cut_free[i % 4] = [tok]
                if self.order is not self.asked:
                    while self.n_cut <= i + 4 and self.n_cut < len(self.order):
                        self.split()

        W = Weights([])

        def jobs_of(name, idx, kt):
            return [(name, idx, k0, min(8, kt - k0)) for k0 in range(0, kt, 8)]

        def dense(job, X_, chunks, ring):
            (name, idx, kt), evac = job
            bb = [ring.take() for _ in chunks]
            specs = jobs_of(name, idx, kt)
            for s, spec in enumerate(specs):
                i, a, b_, toks = W.get(spec)
                n = 0
                for c, (c0, cn) in enumerate(chunks):
                    for k in range(spec[3]):
                        kk = spec[2] + k
                        first, last = kk == 0, kk == kt - 1
                        w1, w2 = a[:, k * P:k * P + P], b_[:, k * P:k * P + P]
                        o = bb[c].ap[:, 0:cn]
                        dep = [toks, X_.tok(kk, c)] + ([bb[c].old] if first else [])
                        pe(mm(o, w1, X_.hi(kk, c0, cn), first, False), dep)
                        pe(mm(o, w2, X_.hi(kk, c0, cn), False, False))
                        end = k == spec[3] - 1
                        t = pe(mm(o, w1, X_.lo(kk, c0, cn), False, last), inc=end)
                        n += 1
                        if n % 2 == 0 and not (end and c == len(chunks) - 1):
                            yield
                    if s == len(specs) - 1:
                        bb[c].free = evac(c, c0, cn, bb[c].ap[:, 0:cn], t)
                        bb[c].free = list(flat([bb[c].free]))
                W.done(i, t)
                yield

        def dense_group(jobs, X_, chunks, ring, mid):
            bb = [[ring.take() for _ in chunks] for _ in jobs]
            got = [W.get(jobs_of(j[0][0], j[0][1], 8)[0]) for j in jobs]
            toks_end = {}
            for k in range(KT):
                for n, (i, a, b_, toks) in enumerate(got):
                    for c, (c0, cn) in enumerate(chunks):
                        o = bb[n][c].ap[:, 0:cn]
                        w1, w2 = a[:, k * P:k * P + P], b_[:, k * P:k * P + P]
                        pe(mm(o, w1, X_.hi(k, c0, cn), k == 0, False), toks, X_.tok(k, c), bb[n][c].old if k == 0 else None)
                        pe(mm(o, w2, X_.hi(k, c0, cn), False, False))
                        toks_end[n, c] = pe(mm(o, w1, X_.lo(k, c0, cn), False, k == 7), inc=k == 7)
            mid()
            for n, j in enumerate(jobs):
                for c, (c0, cn) in enumerate(chunks):
                    bb[n][c].free = list(flat([j[1](c, c0, cn, bb[n][c].ap[:, 0:cn], toks_end[n, c])]))
                W.done(got[n][0], toks_end[n, len(chunks) - 1])

        def run(gen):
            for _ in gen:
                pass

        class Operand:
            def __init__(self, hi, lo):
                self.h, self.l, self.t = hi, lo, {}

            def hi(self, k, c0, cn):
                return self.h[:, k, c0:c0 + cn]

            def lo(self, k, c0, cn):
                return self.l[:, k, c0:c0 + cn]

            def tok(self, k, c):
                return self.t.get((k, c), self.t.get(k))

        U = Operand(uh, ul)
        G = Operand(gh, gl)
        OB = Operand(obh, obl)

        ffn_ring = Ring([banks[i] for i in range(6)])
        mix_ring = Ring([banks[i] for i in range(3)])

        state = {"acc": [], "rb0": [], "rb1": [], "rt": [], "u": [], "x": [], "hold": []}

        def square_into_acc(m, src, tok, cols, scale=1.0):
            if m == 0:
                t = act(fn(acc[:, cols], src, ACT.Square, scale=scale), tok, state["acc"])
                return t, t
            bq = temps.take()
            t = act(fn(bq.ap[:, cols], src, ACT.Square, scale=scale), tok, bq.old)
            t2 = pool(tt(acc[:, cols], acc[:, cols], bq.ap[:, cols], ADD), t, state["accw"])
            bq.free = [t2]
            return t, t2

        def rstd(which, t_acc, blk2, factor=1.0):
            tiles = [0, 1, 2, 3, 4] if blk2 else [1, 2, 3, 4]
            j0 = tiles[0]
            b6, b7 = banks[6], banks[7]
            for j in tiles:
                q0 = 0 if j == 0 else X0 + P * (j - 1)
                t = pe(mm(b6.ap[:, j:j + 1], acc[:, q0:q0 + P], ones[:, 0:1], True, True), t_acc, t_on, b6.free,
                       inc=True)
            state["acc"] = [t]
            sd, rt = small[:, 16 + j0:21], small[:, 8 + j0:13]
            t = act(fn(sd, b6.ap[:, j0:5], ACT.Sqrt, bias=eps, scale=1.0 / D), t, t_eps)
            t_rt = dve(rcp(rt, sd), t, state["rt"])
            dg = temps.take()
            dt = []
            for j in tiles:
                n = 16 if j == 0 else P
                q0 = 0 if j == 0 else X0 + P * (j - 1)
                dt.append(dve(ts(dg.ap[0:n, q0:q0 + n], ident[0:n, 0:n], small[0:n, 8 + j:9 + j], None, MUL), t_rt,
                              dg.old, t_id))
            tb_ = pe(mm(b7.ap[:, :], ones[:, :], dg.ap[:, X0:TW], True, True), dt, b7.free, inc=True)
            tw = act(fn(rb[:, which, X0:TW], b7.ap[:, :], ACT.Copy, scale=factor), tb_, state[f"rb{which}"])
            b7.free = [tw]
            b6.free = [t]
            out = [tw]
            if blk2:
                tb_ = pe(mm(b6.ap[:, 64:80], ones[0:16, :], dg.ap[0:16, 0:16], True, True), dt, t, inc=True)
                tw = act(fn(rb[:, which, 0:X0], b6.ap[:, 64:80], ACT.Copy, scale=factor), tb_)
                b6.free = [tw]
                out.append(tw)
            dg.free = [tb_]
            return out, t_rt

        def prep(m, gain, tok, cols):
            g = gain(m)
            t1 = act(fn(uh[:, m, cols], h[:, m, cols], ACT.Identity, scale=g), tok, state["u"])
            t2 = dve(stt(ul[:, m, cols], h[:, m, cols], g, uh[:, m, cols], MUL, SUB), t1, state["u"])
            U.t[m] = [t1, t2]
            ta, tb_ = square_into_acc(m, h[:, m, cols], tok, cols)
            state["accw"] = tb_
            return tb_, [t1, t2, ta]

        def residual_and_prep(y, y_toks, rb_toks, gain, cols):
            last = None
            reads = []
            for m in range(KT):
                bq = temps.take()
                t = dve(tt(bq.ap[:, cols], y[:, m, cols], rb[:, 1, cols], MUL), y_toks[m], rb_toks, bq.old)
                t2 = pool(tt(h[:, m, cols], h[:, m, cols], bq.ap[:, cols], ADD), t)
                bq.free = [t2]
                reads.append(t)
                state["u"] = state["u"] + [t] if y is y_u else state["u"]
                last, _ = prep(m, gain, t2, cols)
            state["rb1"] = reads
            return last, reads

        def ffn(w, l, which, cols, chunks, blk2, next_gain, post):
            z, rbt = {}, {}
            t_acc = state["last"]

            def mid():
                rbt["t"], t_rt = rstd(0, t_acc, blk2)
                state["rt"] = []

            def gate_evac(f):
                def evac(c, c0, cn, ps, tok):
                    if c == 0:
                        z[f] = temps.take()
                        z[f].t = {}
                    a = z[f].ap[:, c0:c0 + cn]
                    t1 = dve(tt(a, ps, rb[:, 0, c0:c0 + cn], MUL), tok, rbt["t"], z[f].old)
                    t2 = act(fn(a, a, ACT.Silu), t1)
                    z[f].t[c] = pool(tt(a, a, rb[:, 0, c0:c0 + cn], MUL), t2)
                    state["rb0"] = [z[f].t[c]]
                    return t1
                return evac

            def up_evac(f):
                def evac(c, c0, cn, ps, tok):
                    bq = temps.take()
                    a = bq.ap[:, c0:c0 + cn]
                    t1 = dve(tt(a, ps, z[f].ap[:, c0:c0 + cn], MUL), tok, z[f].t[c], bq.old)
                    t2 = act(fn(gh[:, f, c0:c0 + cn], a, ACT.Copy), t1, state["x"])
                    t3 = dve(tt(gl[:, f, c0:c0 + cn], a, gh[:, f, c0:c0 + cn], SUB), t2, state["x"])
                    bq.free = [t2, t3]
                    if c == len(chunks) - 1:
                        z[f].free = [t1]
                    G.t[f, c] = [t2, t3]
                    return t1
                return evac

            jobs = []
            for f in range(FT):
                jobs.append((("gu", (w, f), 8), gate_evac(f)))
                jobs.append((("gu", (w, FT + f), 8), up_evac(f)))
            G.t = {}
            dense_group(jobs[:3], U, chunks, ffn_ring, mid)
            for j in jobs[3:]:
                run(dense(j, U, chunks, ffn_ring))
            state["u"] = [(pe.sem, pe.count)]
            y_toks = {}
            wr = {}

            def down_evac(m):
                def evac(c, c0, cn, ps, tok):
                    cs = slice(c0, c0 + cn)
                    if post is None:
                        t1 = dve(tt(h[:, m, cs], ps, h[:, m, cs], ADD), tok)
                        wr[m, c] = t1
                        if c == len(chunks) - 1:
                            _, t3 = square_into_acc(m, h[:, m, cols], [wr[m, i] for i in range(len(chunks))], cols)
                            state["accw"] = t3
                            wr["last"] = t3
                        return t1
                    ta, tb_ = square_into_acc(m, ps, tok, cs)
                    state["accw"] = tb_
                    t2 = act(fn(y_u[:, m, cs], ps, ACT.Identity, scale=post(m)), tok, state["u"])
                    y_toks[m] = [t2]
                    wr["last"] = tb_
                    return [ta, t2]
                return evac

            for m in range(KT):
                run(dense((("dn", (w, m), FT), down_evac(m)), G, chunks, ffn_ring))
            state["x"] = [(pe.sem, pe.count)]
            if post is None:
                state["last"] = wr["last"]
                return
            rbt2, _ = rstd(1, wr["last"], blk2, 0.5)
            if next_gain is None:
                state["y"] = (y_toks, rbt2)
                return
            state["last"], _ = residual_and_prep(y_u, y_toks, rbt2, next_gain, cols)

        s_banks = [banks[4], banks[5]]
        o_bank = banks[3]
        pt_ring = Ring([banks[6], banks[7]])
        spare = slice(64, 64 + 8 * 16)

        class Filler:

            def __init__(self):
                self.items, self.done, self.active, self.pair = [], set(), None, 0

            def add(self, name, gen, pair=0):
                self.items.append((name, gen, pair))

            def tick(self, n=1):
                while n > 0:
                    if self.active is None:
                        ok = [i for i in self.items if i[2] <= self.pair + 1]
                        if not ok:
                            return
                        self.active = ok[0]
                        self.items.remove(ok[0])
                    if next(self.active[1], "end") == "end":
                        self.done.add(self.active[0])
                        self.active = None
                    else:
                        n -= 1

            def finish(self, name=None):
                if name is None:
                    self.pair = 99
                while (self.items or self.active) and (name is None or name not in self.done):
                    self.tick()

            def need(self, pair, name):
                self.pair = pair
                if pair:
                    self.finish(name)

        def ktok(i):
            return (0, 16) if i == 0 else (X0 + P * (i - 1), P)

        def attention(units, smax, pv, filler, ticks, lag=2):
            pend = []

            def stage2(u, info):
                x, j, kts = u
                e_buf, e_tok = info
                qn = 16 if j == 0 else P
                big = [i for i in kts if i > 0]
                frees = []
                if 0 in kts:
                    bk = pt_ring.take()
                    t = pe(tr(bk.ap[0:16, 0:qn], e_buf.ap[0:qn, 0:16], ident[0:qn, 0:qn]), e_tok, bk.old, t_id,
                           inc=True)
                    dst = ptm[:, :] if j == 0 else PT[0:16, 0, P * (j - 1):P * j]
                    t2 = act(fn(dst, bk.ap[0:16, 0:qn], ACT.Copy), t, state["ptm"] if j == 0 else state["pt"])
                    bk.free = [t2]
                    pt_tok[x, j, 0] = t2
                    frees.append(t)
                if big and j > 0:
                    bk = pt_ring.take()
                    for i in big:
                        k0, kn = ktok(i)
                        t = pe(tr(bk.ap[:, P * (i - 1):P * i], e_buf.ap[:, k0:k0 + kn], ident[:, :]), e_tok, bk.old,
                               t_id, inc=i == big[-1])
                    a, z_ = big[0], big[-1] + 1
                    t2 = act(fn(PT[:, a:z_, P * (j - 1):P * j],
                                bk.ap[:, P * (a - 1):P * (z_ - 1)].rearrange("p (i q) -> p i q", q=P), ACT.Copy), t,
                             state["pt"])
                    bk.free = [t2]
                    pt_tok[x, j, 1] = t2
                    frees.append(t)
                e_buf.free = frees
                if j == 0:
                    pv(x, True)

            filler.pair = 0
            pt_tok = {}
            attention.pt_tok = pt_tok
            state.setdefault("ptm", [])
            queue = []
            for n, u in enumerate(units):
                queue.append((u, smax(u)))
                filler.tick(ticks)
                if len(queue) > lag:
                    u2, info = queue.pop(0)
                    stage2(u2, info)
                    if u2[1] == 4:
                        filler.tick(1)
                        pv(u2[0], False)
            for u2, info in queue:
                filler.tick(1)
                stage2(u2, info)
                if u2[1] == 4:
                    filler.tick(1)
                    pv(u2[0], False)

        def scores(q, kh, kl, j, keys, blk2, which, deps):
            q0 = 0 if j == 0 else X0 + P * (j - 1)
            k0, k1 = keys
            if blk2:
                off = 2048 + 496
                segs = [(a, b_) for a, b_ in ((k0, min(k1, X0)), (max(k0, X0), k1)) if a < b_]
                olds = [s_banks[0].free, s_banks[1].free]
            else:
                off = 2048 + 512 * which - X0
                segs = [(k0, k1)]
                olds = [s_banks[which].free]
            for a, b_ in segs:
                o = PS[:, off + a:off + b_]
                pe(mm(o, q[:, q0:q0 + P], kh[:, a:b_], True, False), deps, olds)
                t = pe(mm(o, q[:, q0:q0 + P], kl[:, a:b_], False, True), inc=True)
            return PS[:, off + k0:off + k1], t

        def s_free(blk2, which, toks):
            if blk2:
                s_banks[0].free = s_banks[1].free = toks
            else:
                s_banks[which].free = toks

        unit_no = [0]

        def sm(i):
            c = 64 + (unit_no[0] % 8) * 16 + i
            return small[:, c:c + 1]

        def normal(e, keys_ap, neg, t_neg, t_e, sink, rows=P):
            r = slice(0, rows)
            l_, d_, es = sm(2)[r], sm(3)[r], sm(4)[r]
            t1 = act(fn(keys_ap, e, ACT.Exp, bias=neg[r], accum=l_), t_neg, t_e)
            dep = [t1]
            if sink is not None:
                t2 = act(fn(es, sink[r], ACT.Exp, bias=neg[r]), t_neg)
                t3 = dve(tt(l_, l_, es, ADD), t1, t2)
                dep = [t3]
            t4 = dve(rcp(d_, l_), dep)
            return d_, t4, t1

        def build_stack(pairname, t_src, tok, slots, kind, cols, free):
            toks = {}
            reads = []
            for hh in range(2):
                own = slice(64 * hh, 64 * hh + 64)
                oth = slice(64 - 64 * hh, 128 - 64 * hh)
                src = t_src[own, cols]
                if kind == "q":
                    s = slots[hh]
                    t1 = act(fn(stk[own, s, cols], src, ACT.Copy), tok, free)
                    t2 = dve(tt(stk[oth, s, cols], src, stk[own, s, cols], SUB), t1, free)
                    toks[hh] = [t1, t2]
                    reads += [t1, t2]
                else:
                    a, b_ = slots[hh]
                    t1 = act(fn(stk[own, a, cols], src, ACT.Copy), tok, free)
                    t2 = act(fn(stk[oth, a, cols], src, ACT.Copy), tok, free)
                    t3 = dve(tt(stk[own, b_, cols], src, stk[own, a, cols], SUB), t1, free)
                    t4 = dve(tt(stk[oth, b_, cols], src, stk[own, a, cols], SUB), t1, free)
                    toks[hh] = [t1, t2, t3, t4]
                    reads += toks[hh]
            return toks, reads

        def mix(l, blk2, chunks, cols, gain_next):
            xt = state["x"]
            rbt = {}
            t_acc = state["last"]
            branch_mats = "wbr"
            win = "win2" if blk2 else "win"
            tiles = [0, 1, 2, 3, 4] if blk2 else [1, 2, 3, 4]

            def widx(i):
                return (i,) if blk2 else (l, i)

            def mid():
                rbt["t"], rbt["rt"] = rstd(0, t_acc, blk2)
                state["rt"] = []

            stack_tok = {}
            stack_free = {}

            def to_stack(key, slots, kind, rope, free):
                st = {}

                def evac(c, c0, cn, ps, tok):
                    cs = slice(c0, c0 + cn)
                    if c == 0:
                        st["b"] = temps.take()
                        st["t"] = []
                    bq = st["b"]
                    if kind == "q":
                        t1 = dve(stt(bq.ap[:, cs], ps, 0.125, rb[:, 0, cs], MUL, MUL), tok, rbt["t"], bq.old)
                    else:
                        t1 = dve(tt(bq.ap[:, cs], ps, rb[:, 0, cs], MUL), tok, rbt["t"], bq.old)
                    st["t"].append(t1)
                    state["rb0"] = [t1]
                    if c == len(chunks) - 1:
                        src, ts_ = bq.ap, st["t"]
                        if rope:
                            b2 = temps.take()
                            xs = slice(X0, TW)
                            r = []
                            for qd in range(4):
                                a = slice(32 * qd, 32 * qd + 32)
                                o = slice(32 * (qd ^ 1), 32 * (qd ^ 1) + 32)
                                eng = pool if qd % 2 else dve
                                r.append(eng(tt(b2.ap[o, xs], bq.ap[a, xs], sin[a, :], MUL), ts_, b2.old, rbt["tab"]))
                            t2 = dve(tt(bq.ap[:, xs], bq.ap[:, xs], cos[:, :], MUL), r, rbt["tab"])
                            t3 = dve(tt(bq.ap[:, xs], bq.ap[:, xs], b2.ap[:, xs], ADD), t2, r)
                            b2.free = [t3]
                            ts_ = [t3]
                        toks, reads = build_stack(key, src, ts_, slots, kind, cols, free())
                        bq.free = reads
                        stack_tok[key] = toks
                    return t1
                return evac

            def gate_job(n, m, dst, tok_box):
                base = 23 if blk2 else 22

                def evac(c, c0, cn, ps, tok):
                    cs = slice(c0, c0 + cn)
                    if c == 0 and callable(dst):
                        tok_box["b"] = dst()
                    bq = tok_box["b"]
                    t1 = dve(tt(bq.ap[:, cs], ps, rb[:, 0, cs], MUL), tok, rbt["t"], bq.old)
                    state["rb0"] = [t1]
                    bias = 0.0 if blk2 else par[:, HB + 24 * l + 8 * n + m:HB + 24 * l + 8 * n + m + 1]
                    tok_box[c] = act(fn(bq.ap[:, cs], bq.ap[:, cs], ACT.Tanh, bias=bias, scale=0.5), t1, t_hb)
                    return t1
                return ((win, widx(base + 8 * n + m), 8), evac)

            gate_bufs = [Buf(gates[:, i, :]) for i in range(2)]
            macc_tok = {}

            def merge(n, first, last):
                for m in range(KT):
                    box = gate_box[n, m]
                    if m >= 2:
                        run(dense(gate_job(n, m, temps.take, box), U, chunks, mix_ring))

                    def evac(c, c0, cn, ps, tok, m=m, box=box):
                        cs = slice(c0, c0 + cn)
                        dst = macc[:, m, cs]
                        g = box["b"].ap[:, cs]
                        if first:
                            t1 = dve(stt(dst, g, 1.0, ps, ADD, MUL), tok, box[c], xt)
                            t2 = t1
                        else:
                            t1 = dve(stt(g, g, 1.0, ps, ADD, MUL), tok, box[c])
                            t2 = pool(tt(dst, dst, g, ADD), t1, macc_tok[m, c])
                        macc_tok[m, c] = t2
                        if c == len(chunks) - 1:
                            box["b"].free = [macc_tok[m, i] for i in range(len(chunks))]
                        return t1
                    run(dense(((branch_mats, ((2 if blk2 else l), n, m), 4), evac), OB, chunks, mix_ring))
                state["ob"] = [(pe.sem, pe.count)]

            gate_box = {(n, m): {} for n in range(3) for m in range(KT)}
            state["ob"] = xt
            state["pt"] = list(xt)
            state["ptm"] = list(xt)
            state["v"] = list(xt)
            for i in range(2):
                gate_bufs[i].free = list(xt)

            def gate_fill(filler, n):
                for m in range(2):
                    def gen(m=m):
                        gate_bufs[m].old = gate_bufs[m].free
                        gate_bufs[m].free = None
                        gate_box[n, m]["b"] = gate_bufs[m]
                        yield from dense(gate_job(n, m, None, gate_box[n, m]), U, chunks, mix_ring)
                    filler.add(("gate", n, m), gen())

            def values(vname, vidx):
                vb = [o_bank, banks[4], banks[5], banks[6], banks[7]][:len(tiles)]
                olds = [b_.free for b_ in vb]
                for kc in range(4):
                    i, a, b_, toks = W.get((vname, vidx + (kc,), 0, 8))
                    for n, j in enumerate(tiles):
                        q0 = 0 if j == 0 else X0 + P * (j - 1)
                        for k2 in range(2):
                            kk = 2 * kc + k2
                            w1, w2 = a[:, 512 * k2:512 * k2 + 512], b_[:, 512 * k2:512 * k2 + 512]
                            o = vb[n].ap
                            u1, u2 = uh[:, kk, q0:q0 + P], ul[:, kk, q0:q0 + P]
                            pe(mm(o, u1, w1, kk == 0, False), toks, U.tok(kk, 0), olds[n] if kk == 0 else None)
                            pe(mm(o, u1, w2, False, False))
                            t = pe(mm(o, u2, w1, False, kk == 7), inc=k2 == 1)
                        if kc == 3:
                            r = slice(0, 16 if j == 0 else P)
                            t2 = act(fn(V[r, j, :], o[r, :], ACT.Copy, scale=small[r, 8 + j:9 + j]), t, rbt["rt"],
                                     state["v"])
                            vb[n].free = [t2]
                            v_tok.append(t2)
                    W.done(i, t)

            v_tok = []

            def values_from_t(job_idx):
                st = {}

                def evac(c, c0, cn, ps, tok):
                    if c == 0:
                        st["b"] = temps.take()
                        st["t"] = []
                    bq = st["b"]
                    cs = slice(c0, c0 + cn)
                    t1 = dve(tt(bq.ap[:, cs], ps, rb[:, 0, cs], MUL), tok, rbt["t"], bq.old)
                    state["rb0"] = [t1]
                    st["t"].append(t1)
                    if c == len(chunks) - 1:
                        fr = []
                        bk = pt_ring.take()
                        for j in tiles[-4:]:
                            t = pe(tr(bk.ap[:, P * (j - 1):P * j], bq.ap[:, X0 + P * (j - 1):X0 + P * j], ident[:, :]),
                                   st["t"], bk.old, t_id, inc=True)
                        t2 = act(fn(V[:, 1:5, 0:P], bk.ap[:, :].rearrange("p (j d) -> p j d", d=P), ACT.Copy), t,
                                 state["v"])
                        bk.free = [t2]
                        v_tok.append(t2)
                        if blk2:
                            bk = pt_ring.take()
                            t = pe(tr(bk.ap[0:16, 0:P], bq.ap[:, 0:16], ident[:, :]), st["t"], bk.old, inc=True)
                            t2 = act(fn(V[0:16, 0, 0:P], bk.ap[0:16, 0:P], ACT.Copy), t, state["v"])
                            bk.free = [t2]
                            v_tok.append(t2)
                        bq.free = [t]
                    return t1
                return ((win, widx(job_idx), 8), evac)

            def pv_plain(pairs, vcol, plan):
                def pv(x, meta):
                    t_, par_ = pairs(x)
                    rows = slice(64 * par_, 64 * par_ + 64)
                    vc = vcol(x)
                    pt_tok = attention.pt_tok
                    if meta:
                        bk = pt_ring.take()
                        t = pe(mm(bk.ap[:, 0:16], V[0:16, 0, vc], ptm[:, :], True, True), pt_tok[x, 0, 0], v_tok,
                               bk.old, inc=True)
                        state["ptm"] = [t]
                        cs = slice(0, 16)
                        src = bk.ap[rows, 0:16]
                    else:
                        deps = [pt_tok.get((x, j, a)) for j in range(1, 5) for a in range(2)]
                        old = o_bank.free
                        for n, (i, qa, qb_) in enumerate(plan):
                            k0, kn = ktok(i)
                            c0, c1 = P * (qa - 1), P * (qb_ - 1)
                            rr = slice(0, 16) if i == 0 else slice(0, P)
                            t = pe(mm(o_bank.ap[:, c0:c1], V[rr, i, vc], PT[rr, i, c0:c1], n == 0, n == len(plan) - 1),
                                   deps, v_tok, old, inc=n == len(plan) - 1)
                        state["pt"] = [t]
                        cs = slice(X0, TW)
                        src = o_bank.ap[rows, :]
                    t1 = act(fn(obh[rows, t_, cs], src, ACT.Copy), t, state["ob"])
                    t2 = dve(tt(obl[rows, t_, cs], src, obh[rows, t_, cs], SUB), t1, state["ob"])
                    if meta:
                        bk.free = [t1, t2]
                    else:
                        o_bank.free = [t1, t2]
                    OB.t.setdefault(t_, []).extend([t1, t2])
                    state["v"] = [t]
                return pv

            filler = Filler()

            def free_of(key):
                return lambda: stack_free.get(key, list(xt))

            def pair_slots(p):
                s = 6 * (p % 2)
                return [s, s + 3], [(s + 1, s + 2), (s + 4, s + 5)]

            def proj_pair(tag, p, qi, ki, rope):
                qs, ks = pair_slots(p)
                return [((win, widx(qi + p), 8), to_stack((tag, "q", p), qs, "q", rope, free_of(p % 2))),
                        ((win, widx(ki + p), 8), to_stack((tag, "k", p), ks, "k", rope, free_of(p % 2)))]

            def add_proj(filler, tag, p, qi, ki, rope):
                for n, j in enumerate(proj_pair(tag, p, qi, ki, rope)):
                    filler.add((tag, p, n), dense(j, U, chunks, mix_ring), p)

            def done_unit(p, tok):
                stack_free[p % 2] = [tok]

            first_group = {"done": False}

            def start(jobs):
                if not first_group["done"]:
                    dense_group(jobs, U, chunks, ffn_ring, mid)
                    first_group["done"] = True
                else:
                    for j in jobs:
                        run(dense(j, U, chunks, mix_ring))

            if not blk2:
                t_ma = sp.dma(slot("tab0"), ld(maska[:, :], T["c_mask_a"]), xt)
                tb_bufs = [Buf(tb[:, i, :]) for i in range(2)]
                for b_ in tb_bufs:
                    b_.free = list(xt)
                tb_tok = {}

                def load_tb(x):
                    if x >= 8:
                        return
                    bf = tb_bufs[x % 2]
                    th = T["rpb"].tensor
                    base = (l * 8 + x) * 15 * 64 * P + 63
                    dst = bf.ap.rearrange("p (r c) -> p r c", c=64)
                    ta = pool.dma(slot(f"tb{x % 2}"), ld(dst[0:64], bass.AP(th, base + 64 * P, [[127, 64], [64 * P, 14], [1, 64]])),
                                  bf.free)
                    tb2 = pool.dma(slot(f"tb{x % 2}"), ld(dst[64:128], bass.AP(th, base, [[127, 64], [64 * P, 14], [1, 64]])),
                                   bf.free)
                    m_ = maska[:, :].unsqueeze(1).to_broadcast([P, 14, 64])
                    tb_tok[x] = pool(tt(dst, dst, m_, ADD), ta, tb2, t_ma)

                def smax_a(u):
                    x, j, kts = u
                    p, hh = x // 2, x % 2
                    filler.need(p, ("A", p, 1))
                    qs, ks = pair_slots(p)
                    w = unit_no[0] % 2
                    S, ts_ = scores(stk[:, qs[hh], :], stk[:, ks[hh][0], :], stk[:, ks[hh][1], :], j, (X0, TW), False, w,
                                    [stack_tok["A", "q", p][hh], stack_tok["A", "k", p][hh]])
                    done_unit(p, ts_)
                    eb = temps.take()
                    e = eb.ap[:, X0:TW]
                    mx, ng = sm(0), sm(1)
                    off = (6 - 2 * (j - 1)) * 64
                    tbl = tb_bufs[x % 2].ap[:, off:off + 512]
                    t1 = dve(lambda en: en.tensor_tensor_reduce(e, S, tbl, 1.0, LOWEST, ADD, MAX, mx), ts_, eb.old,
                             tb_tok[x])
                    s_free(False, w, [t1])
                    t2 = dve(ts(ng, mx, -1.0, None, MUL), t1)
                    d_, t4, te = normal(e, e, ng, t2, t1, None)
                    t5 = dve(ts(e, e, d_, None, MUL), t4)
                    unit_no[0] += 1
                    if j == 4:
                        tb_bufs[x % 2].free = [t1]
                        load_tb(x + 2)
                    return eb, t5

                load_tb(0)
                load_tb(1)
                jobs = proj_pair("A", 0, 0, 4, False)
                gate_bufs[0].old, gate_bufs[0].free = gate_bufs[0].free, None
                gate_box[0, 0]["b"] = gate_bufs[0]
                jobs.append(gate_job(0, 0, None, gate_box[0, 0]))
                start(jobs)
                values("wv", (l, 0))

                def gen01():
                    gate_bufs[1].old, gate_bufs[1].free = gate_bufs[1].free, None
                    gate_box[0, 1]["b"] = gate_bufs[1]
                    yield from dense(gate_job(0, 1, None, gate_box[0, 1]), U, chunks, mix_ring)

                for p in range(1, 4):
                    add_proj(filler, "A", p, 0, 4, False)
                filler.add("g", gen01())
                units = [(x, j, [1, 2, 3, 4]) for x in range(8) for j in range(1, 5)]
                OB.t = {}
                attention(units, smax_a, pv_plain(lambda x: (x // 2, x % 2), lambda x: slice(P * (x // 2), P * (x // 2) + P),
                                                         [(i, 1, 5) for i in range(1, 5)]), filler, 1)
                filler.finish()
                merge(0, True, False)

                t_a = [(pool.sem, pool.count), (dve.sem, dve.count)]
                tabs = [sp.dma(slot("tab1"), ld(cos[:, :], T["c_cos"]), t_a),
                        sp.dma(slot("tab2"), ld(sin[:, :], T["c_sin"]), t_a),
                        sp.dma(slot("tab3"), ld(maskb[:, :], T["c_mask_b"]), t_a)]
                rbt["tab"] = tabs
                all_free = list(flat([stack_free.get(0), stack_free.get(1)]))
                v_tok.clear()
                kslots = [(8, 9), (10, 11)]
                start([((win, widx(12), 8), to_stack(("B", "k"), kslots, "k", True, lambda: all_free)),
                       ((win, widx(8), 8), to_stack(("B", "q", 0), [0, 1], "q", True, lambda: all_free)),
                       values_from_t(13)])
                bq_free = {1: all_free}
                for p in range(1, 4):
                    filler.add(("B", p, 0), dense(((win, widx(8 + p), 8), to_stack(("B", "q", p), [2 * (p % 2), 2 * (p % 2) + 1],
                               "q", True, (lambda p=p: bq_free.get(p % 2, all_free)))), U, chunks, mix_ring), p)
                gate_fill(filler, 1)

                def smax_b(u):
                    x, j, kts = u
                    p, hh = x // 2, x % 2
                    filler.need(p, ("B", p, 0))
                    head = p + 4 * hh
                    w = unit_no[0] % 2
                    k0, k1 = X0 + P * (kts[0] - 1), X0 + P * kts[-1]
                    S, ts_ = scores(stk[:, 2 * (p % 2) + hh, :], stk[:, kslots[hh][0], :], stk[:, kslots[hh][1], :], j,
                                    (k0, k1), False, w, [stack_tok["B", "q", p][hh], stack_tok["B", "k"][hh]])
                    bq_free[p % 2] = [ts_]
                    eb = temps.take()
                    e = eb.ap[:, k0:k1]
                    mx, ng = sm(0), sm(1)
                    off = P if j == 1 else 0
                    mk = maskb[:, off:off + (k1 - k0)]
                    sink = pcol("sink", l, head)
                    t1 = dve(lambda en: en.tensor_tensor_reduce(e, S, mk, 1.0, sink, ADD, MAX, mx), ts_, eb.old, tabs)
                    s_free(False, w, [t1])
                    t2 = dve(ts(ng, mx, -1.0, None, MUL), t1)
                    d_, t4, te = normal(e, e, ng, t2, t1, sink)
                    t5 = dve(ts(e, e, d_, None, MUL), t4)
                    unit_no[0] += 1
                    return eb, t5

                units = [(x, j, [i for i in (j - 1, j, j + 1) if 1 <= i <= 4]) for x in range(8) for j in range(1, 5)]
                OB.t = {}
                plan = [(i, max(1, i - 1), min(4, i + 1) + 1) for i in range(1, 5)]
                attention(units, smax_b, pv_plain(lambda x: (x // 2, x % 2), lambda x: slice(0, P), plan),
                          filler, 1)
                filler.finish()
                all_free = list(flat([bq_free.get(0), bq_free.get(1), (pe.sem, pe.count)]))
                merge(1, False, False)

                stack_free[0] = stack_free[1] = all_free
                v_tok.clear()
                start(proj_pair("C", 0, 14, 18, True))
                values("wv", (l, 1))
                for p in range(1, 4):
                    add_proj(filler, "C", p, 14, 18, True)
                gate_fill(filler, 2)

                def smax_c(u):
                    x, j, kts = u
                    filler.need(x, ("C", x, 1))
                    qs, ks = pair_slots(x)
                    res = []
                    for s in range(2):
                        S, ts_ = scores(stk[:, qs[s], :], stk[:, ks[s][0], :], stk[:, ks[s][1], :], j, (X0, TW), False, s,
                                        [stack_tok["C", "q", x][s], stack_tok["C", "k", x][s]])
                        eb = temps.take()
                        e = eb.ap[:, X0:TW]
                        ng = sm(1)
                        t1 = dve(lambda en, ng=ng, S=S: en.tensor_reduce(ng, S, AX.X, MAX, negate=True), ts_)
                        d_, t4, te = normal(S, e, ng, t1, [ts_, eb.old], None)
                        s_free(False, s, [te])
                        res.append((eb, e, d_, t4))
                        unit_no[0] += 1
                    done_unit(x, ts_)
                    (e0b, e0, d0, ta), (e1b, e1, d1, tb_) = res
                    t5 = dve(ts(e0, e0, d0, None, MUL), ta)
                    t6 = dve(ts(d1, d1, par[:, NLAM + l:NLAM + l + 1], None, MUL), tb_, t_lamall)
                    t7 = dve(stt(e0, e1, d1, e0, MUL, ADD), t5, t6)
                    e1b.free = [t7]
                    return e0b, t7

                ss = banks[6].ap
                c_state = {}

                def pv_c(x, meta):
                    pt_tok = attention.pt_tok
                    deps = [pt_tok.get((x, j, 1)) for j in range(1, 5)]
                    old = o_bank.free
                    for n, i in enumerate(range(1, 5)):
                        t = pe(mm(o_bank.ap[:, :], V[:, i, P * x:P * x + P], PT[:, i, :], n == 0, n == 3), deps, v_tok,
                               old, inc=n == 3)
                    state["pt"] = [t]
                    state["v"] = [t]
                    t1 = act(fn(obf[:, x, X0:TW], o_bank.ap, ACT.Copy), t, state["ob"])
                    sq = temps.take()
                    t2 = act(fn(sq.ap[:, X0:TW], o_bank.ap, ACT.Square), t, sq.old)
                    o_bank.free = [t1, t2]
                    bk = pt_ring.take()
                    for j in range(4):
                        t = pe(mm(bk.ap[:, j:j + 1], sq.ap[:, X0 + P * j:X0 + P * j + P], ones[:, 0:1], True, True), t2,
                               bk.old, inc=True)
                    sq.free = [t]
                    t3 = act(fn(small[:, 32 + 4 * x:36 + 4 * x], bk.ap[:, 0:4], ACT.Copy), t)
                    bk.free = [t3]
                    c_state[x] = [t1, t3]

                units = [(x, j, [1, 2, 3, 4]) for x in range(4) for j in range(1, 5)]
                OB.t = {}
                attention(units, smax_c, pv_c, filler, 2, 1)
                ta = act(fn(small[:, 32:48], small[:, 32:48], ACT.Sqrt, bias=eps, scale=1.0 / P),
                         [c_state[x] for x in range(4)])
                tb_ = dve(rcp(small[:, 32:48], small[:, 32:48]), ta)
                for x in range(4):
                    dg = temps.take()
                    dt = [dve(ts(dg.ap[:, X0 + P * j:X0 + P * j + P], ident[:, :], small[:, 32 + 4 * x + j:33 + 4 * x + j],
                                 None, MUL), tb_, dg.old) for j in range(4)]
                    filler.tick(1)
                    bk = pt_ring.take()
                    t = pe(mm(bk.ap[:, :], ones[:, :], dg.ap[:, X0:TW], True, True), dt, bk.old, inc=True)
                    dg.free = [t]
                    tp = temps.take()
                    t1 = dve(stt(tp.ap[:, X0:TW], obf[:, x, X0:TW], par[:, SUBG + l:SUBG + l + 1], bk.ap, MUL, MUL), t,
                             tp.old, c_state[x])
                    bk.free = [t1]
                    t2 = act(fn(obh[:, x, X0:TW], tp.ap[:, X0:TW], ACT.Copy), t1)
                    t3 = dve(tt(obl[:, x, X0:TW], tp.ap[:, X0:TW], obh[:, x, X0:TW], SUB), t2, state["ob"])
                    tp.free = [t2, t3]
                    OB.t[x] = [t2, t3]
                filler.finish()
                merge(2, False, True)

            if blk2:
                t_oh = sp.dma(slot("tab0"), ld(onehot[:, :], T["c_onehot"]), xt)
                t_re = sp.dma(slot("tab1"), ld(relt[:, :], T["rel"]), xt)
                t_ms = sp.dma(slot("tab2"), ld(masks[:, :], T["c_mask_s"]), xt)
                bk = banks[7]
                t = pe(mm(bk.ap[0:8, 0:384], relt[:, :], onehot[:, :], True, True), t_oh, t_re, bk.free, inc=True)
                t = act(fn(relv[:, :], bk.ap[0:8, 0:384], ACT.Copy), t)
                bk.free = [t]
                t_rv = pool.dma(slot("rv"), ld(RELV, relv[:, :].unsqueeze(1).to_broadcast([8, P, 384])), t)
                sbufs = [Buf(sbias[:, i, :]) for i in range(2)]
                for b_ in sbufs:
                    b_.free = list(xt)
                sb_tok = {}

                def head_of(x):
                    return x // 2 + 4 * (x % 2)

                def load_sb(x):
                    if x >= 8:
                        return
                    bf = sbufs[x % 2]
                    src = bass.AP(RELV.tensor, head_of(x) * P * 384 + 127, [[383, P], [1, 256]])
                    t = pool.dma(slot(f"tb{x % 2}"), ld(bf.ap, src), bf.free, t_rv)
                    sb_tok[x] = pool(tt(bf.ap, bf.ap, masks[:, :], ADD), t, t_ms)

                load_sb(0)
                load_sb(1)
                kslots = [(8, 9), (10, 11)]
                jobs = [((win, widx(4), 8), to_stack(("S", "k"), kslots, "k", False, lambda: xt)),
                        ((win, widx(0), 8), to_stack(("S", "q", 0), [0, 1], "q", False, lambda: xt)),
                        values_from_t(5)]
                start(jobs)
                sq_free = {}
                for p in range(1, 4):
                    filler.add(("S", p, 0), dense(((win, widx(p), 8), to_stack(("S", "q", p), [2 * (p % 2), 2 * (p % 2) + 1],
                               "q", False, (lambda p=p: sq_free.get(p % 2, xt)))), U, chunks, mix_ring), p)
                gate_fill(filler, 0)

                def smax_s(u):
                    x, j, kts = u
                    p, hh = x // 2, x % 2
                    filler.need(p, ("S", p, 0))
                    head = head_of(x)
                    rows = 16 if j == 0 else P
                    k0, k1 = ktok(kts[0])[0], sum(ktok(kts[-1]))
                    S, ts_ = scores(stk[:, 2 * (p % 2) + hh, :], stk[:, kslots[hh][0], :], stk[:, kslots[hh][1], :], j,
                                    (k0, k1), True, 0, [stack_tok["S", "q", p][hh], stack_tok["S", "k"][hh]])
                    sq_free[p % 2] = [ts_]
                    eb = temps.take()
                    r = slice(0, rows)
                    e = eb.ap[r, k0:k1]
                    mx, ng = sm(0), sm(1)
                    off = P if j == 0 else (256 - (k1 - k0))
                    bias = sbufs[x % 2].ap[r, off:off + (k1 - k0)]
                    sink = pcol("sink", 2, head)
                    t1 = dve(lambda en: en.tensor_tensor_reduce(e, S[r], bias, 1.0, sink[r], ADD, MAX, mx[r]), ts_, eb.old,
                             sb_tok[x])
                    s_free(True, 0, [t1])
                    t2 = dve(ts(ng[r], mx[r], -1.0, None, MUL), t1)
                    d_, t4, te = normal(e, e, ng, t2, t1, sink, rows)
                    t5 = dve(ts(e, e, d_, None, MUL), t4)
                    unit_no[0] += 1
                    if j == 4:
                        sbufs[x % 2].free = [t1]
                        load_sb(x + 2)
                    return eb, t5

                units = [(x, j, [i for i in (j - 1, j) if i >= 0]) for x in range(8) for j in range(5)]
                OB.t = {}
                attention(units, smax_s, pv_plain(lambda x: (x // 2, x % 2), lambda x: slice(0, P),
                          [(0, 1, 2), (1, 1, 3), (2, 2, 4), (3, 3, 5), (4, 4, 5)]), filler, 1)
                filler.finish()
                merge(0, True, False)

                all_free = [(pe.sem, pe.count)]
                stack_free[0] = stack_free[1] = all_free
                v_tok.clear()
                t_prev = [(dve.sem, dve.count), (pool.sem, pool.count)]
                fx = {}

                def fl_evac(c, c0, cn, ps, tok):
                    cs = slice(c0, c0 + cn)
                    if c == 0:
                        fx["z"] = temps.take()
                    z_ = fx["z"].ap[0:8, cs]
                    t1 = dve(tt(z_, ps[0:8, :], rb[0:8, 0, cs], MUL), tok, rbt["t"], fx["z"].old)
                    state["rb0"] = [t1]
                    fx[c] = t1
                    return t1

                def log_sigmoid(x_ap, a_ap, b_ap, s_ap, p_ap, out_ap, tok):
                    t = dve(ts(a_ap, x_ap, -1.0, None, MUL), tok)
                    t = dve(tt(a_ap, a_ap, x_ap, MAX), t)
                    t = act(fn(a_ap, a_ap, ACT.Exp, scale=-1.0), t)
                    t = dve(ts(b_ap, a_ap, 2.0, None, ADD), t)
                    t = dve(rcp(b_ap, b_ap), t)
                    t = dve(tt(s_ap, a_ap, b_ap, MUL), t)
                    t = dve(tt(b_ap, s_ap, s_ap, MUL), t)
                    t = dve(ts(p_ap, b_ap, 1.0 / 17, 1.0 / 15, MUL, ADD), t)
                    for k in (13, 11, 9, 7, 5, 3, 1):
                        t = dve(tt(p_ap, p_ap, b_ap, MUL), t)
                        t = dve(ts(p_ap, p_ap, 1.0 / k, None, ADD), t)
                    t = dve(tt(p_ap, p_ap, s_ap, MUL), t)
                    t = dve(ts(a_ap, x_ap, 0.0, None, MIN), t)
                    return dve(stt(out_ap, p_ap, -2.0, a_ap, MUL, ADD), t)

                start([((win, widx(14), 8), fl_evac)])
                z_ = fx["z"].ap[0:8, :]
                t = dve(ts(z_, z_, par[0:8, PCOLS["foxb", 2]:PCOLS["foxb", 2] + 1], None, ADD), fx[0], fx[1])
                ta_, tb2, tc_, td_ = [temps.take() for _ in range(4)]
                t = log_sigmoid(z_, ta_.ap[0:8, :], tb2.ap[0:8, :], tc_.ap[0:8, :], td_.ap[0:8, :], z_,
                                [t, ta_.old, tb2.old, tc_.old, td_.old])
                t = dve(lambda e: e.memset(ta_.ap[0:8, :], 1.0), t)
                t_cum = dve(lambda e: e.tensor_tensor_scan(cumt[:, :], ta_.ap[0:8, :], z_, 0.0, MUL, ADD), t, t_prev)
                for b_ in (fx["z"], ta_, tb2, tc_, td_):
                    b_.free = [t_cum]
                t_cs = pool.dma(slot("rv"), ld(CUM, cumt[:, :]), t_cum)
                bk = pt_ring.take()
                for j in range(5):
                    q0 = 0 if j == 0 else X0 + P * (j - 1)
                    t = pe(tr(bk.ap[:, 8 * j:8 * j + 8], cumt[:, q0:q0 + P], ident[0:8, 0:8]), t_cum, bk.old, inc=True)
                t_ci = act(fn(ci[:, :, :], bk.ap[:, 0:40].rearrange("p (j h) -> p j h", h=8), ACT.Copy), t, t_prev)
                bk.free = [t_ci]
                cbufs = [Buf(cumb[:, i, :]) for i in range(2)]
                for b_ in cbufs:
                    b_.free = list(t_prev)
                cb_tok = {}

                def load_cb(x):
                    if x >= 8:
                        return
                    src = bass.AP(CUM.tensor, x * TW, [[0, P], [1, TW]])
                    cb_tok[x] = pool.dma(slot(f"tb{x % 2}"), ld(cbufs[x % 2].ap, src), cbufs[x % 2].free, t_cs)

                load_cb(0)
                load_cb(1)
                start(proj_pair("F", 0, 6, 10, False))
                values("wv2", ())
                for p in range(1, 4):
                    add_proj(filler, "F", p, 6, 10, False)
                gate_fill(filler, 1)

                def smax_f(u):
                    x, j, kts = u
                    p, hh = x // 2, x % 2
                    filler.need(p, ("F", p, 1))
                    qs, ks = pair_slots(p)
                    rows = 16 if j == 0 else P
                    r = slice(0, rows)
                    k1 = sum(ktok(j))
                    S, ts_ = scores(stk[:, qs[hh], :], stk[:, ks[hh][0], :], stk[:, ks[hh][1], :], j, (0, k1), True, 0,
                                    [stack_tok["F", "q", p][hh], stack_tok["F", "k", p][hh]])
                    done_unit(p, ts_)
                    eb = temps.take()
                    e = eb.ap[r, 0:k1]
                    ng = sm(1)
                    t1 = dve(stt(e, S[r], ci[r, j, x:x + 1], cbufs[x % 2].ap[r, 0:k1], ADD, SUB), ts_, eb.old, t_ci,
                             cb_tok[x])
                    s_free(True, 0, [t1])
                    dg_ = eb.ap[r, k1 - rows:k1]
                    t2 = dve(tt(dg_, dg_, maskt[r, 0:rows], ADD), t1, t_mt)
                    t3 = dve(lambda en: en.tensor_reduce(ng[r], e, AX.X, MAX, negate=True), t2)
                    d_, t4, te = normal(e, e, ng, t3, t2, None, rows)
                    t5 = dve(ts(e, e, d_, None, MUL), t4)
                    unit_no[0] += 1
                    if j == 4:
                        cbufs[x % 2].free = [t1]
                        load_cb(x + 2)
                    return eb, t5

                units = [(x, j, list(range(j + 1))) for x in range(8) for j in range(5)]
                OB.t = {}
                attention(units, smax_f, pv_plain(lambda x: (x // 2, x % 2), lambda x: slice(P * (x // 2), P * (x // 2) + P),
                          [(0, 1, 5), (1, 1, 5), (2, 2, 5), (3, 3, 5), (4, 4, 5)]), filler, 1)
                filler.finish()
                t_att = [(pe.sem, pe.count), (act.sem, act.count), (dve.sem, dve.count)]
                merge(1, False, False)

                lc = 57
                t = log_sigmoid(par[:, PCOLS["lam", 2]:PCOLS["lam", 2] + 4], small[:, 208:212], small[:, 212:216],
                                small[:, 216:220], small[:, 220:224], small[:, 224:228], t_par)
                t = dve(ts(par[:, C8:C8 + 4], small[:, 224:228], 8.0, None, MUL), t)
                t_c8 = dve(ts(par[:, NC8:NC8 + 4], small[:, 224:228], -8.0, None, MUL), t)
                lwt = lru[:, 18:20, 0:512]
                t_lw = sp.dma(slot("tab3"), ld(lwt, T["lruw"].rearrange("p (a n) -> p a n", a=2)), t_att)
                lr = {}
                t_z = dve(lambda e: e.memset(lru[:, 0:4, 0:3], 0.0), t_att)

                def xc_evac(m):
                    def evac(c, c0, cn, ps, tok):
                        t1 = dve(tt(lru[:, m, 3 + c0:3 + c0 + cn], ps, rb[:, 0, c0:c0 + cn], MUL), tok, rbt["t"], t_att)
                        state["rb0"] = [t1]
                        lr["x", m, c] = t1
                        return t1
                    return evac

                for m in range(4):
                    run(dense(((win, widx(15 + m), 8), xc_evac(m)), U, chunks, mix_ring))
                    cw = PCOLS["convw", 2]
                    cv = lru[:, 4 + m, 0:TW]
                    t = dve(ts(cv, lru[:, m, 0:TW], par[:, cw + m:cw + m + 1], pcol("convb", 2, m), MUL, ADD), t_z,
                            lr["x", m, 0], lr["x", m, 1])
                    for i in range(1, 4):
                        t = dve(stt(cv, lru[:, m, i:i + TW], par[:, cw + 4 * i + m:cw + 4 * i + m + 1], cv, MUL, ADD), t)
                    lr["c", m] = t
                for m in range(4):
                    for a, (name, row) in enumerate((("br", 8), ("bi", 12))):
                        for c, (c0, cn) in enumerate(chunks):
                            bk = mix_ring.take()
                            t = pe(mm(bk.ap[:, 0:cn], lwt[:, a, P * m:P * m + P], lru[:, 4 + m, c0:c0 + cn], True, True),
                                   t_lw, lr["c", m], bk.old, inc=True)
                            t1 = act(fn(lru[:, row + m, c0:c0 + cn], bk.ap[:, 0:cn], ACT.Sigmoid,
                                        bias=pcol(name, 2, m)), t, t_att)
                            bk.free = [t1]
                            lr[name, m] = t1
                for m in range(4):
                    ga, gb = temps.take(), temps.take()
                    r_ = lru[:, 8 + m, 0:TW]
                    t1 = act(fn(ga.ap, r_, ACT.Tanh, scale=par[:, NC8 + m:NC8 + m + 1]), lr["br", m], t_c8, ga.old)
                    t2 = act(fn(r_, r_, ACT.Exp, scale=par[:, C8 + m:C8 + m + 1]), t1)
                    t3 = dve(tt(gb.ap, r_, r_, MUL), t2, gb.old)
                    t4 = dve(stt(gb.ap, gb.ap, 1.0, ga.ap, ADD, MUL), t3)
                    t5 = dve(tt(lru[:, 12 + m, 0:TW], lru[:, 12 + m, 0:TW], lru[:, 4 + m, 0:TW], MUL), lr["bi", m])
                    t6 = act(fn(gb.ap, gb.ap, ACT.Sqrt), t4)
                    t7 = dve(tt(gb.ap, gb.ap, lru[:, 12 + m, 0:TW], MUL), t5, t6)
                    t8 = dve(lambda e, m=m, gb=gb, r_=r_: e.tensor_tensor_scan(lru[:, 12 + m, 0:TW], r_, gb.ap, 0.0, MUL, ADD), t7)
                    ga.free, gb.free = [t4], [t8]
                    lr["h", m] = t8
                OB.t = {}

                def yc_evac(m):
                    def evac(c, c0, cn, ps, tok):
                        y_ = lru[:, 16 + m % 2, 0:TW]
                        t1 = dve(tt(y_[:, c0:c0 + cn], ps, rb[:, 0, c0:c0 + cn], MUL), tok, rbt["t"], t_att,
                                 lr.get(("y", m - 2)))
                        state["rb0"] = [t1]
                        lr["yt", m, c] = t1
                        if c == 1:
                            b1 = temps.take()
                            t2 = dve(tt(b1.ap, y_, y_, MUL), lr["yt", m, 0], t1, b1.old)
                            t3 = dve(ts(b1.ap, b1.ap, 0.044715, 1.0, MUL, ADD), t2)
                            t4 = dve(tt(b1.ap, b1.ap, y_, MUL), t3)
                            t5 = act(fn(b1.ap, b1.ap, ACT.Tanh, scale=math.sqrt(2.0 / math.pi)), t4)
                            t6 = dve(stt(b1.ap, b1.ap, 1.0, y_, ADD, MUL), t5)
                            t7 = dve(stt(b1.ap, b1.ap, 0.5, lru[:, 12 + m, 0:TW], MUL, MUL), t6, lr["h", m])
                            t8 = act(fn(obh[:, m, :], b1.ap, ACT.Copy), t7, state["ob"])
                            t9 = dve(tt(obl[:, m, :], b1.ap, obh[:, m, :], SUB), t8, state["ob"])
                            b1.free = [t8, t9]
                            lr["y", m] = t6
                            OB.t[m] = [t8, t9]
                        return t1
                    return evac

                for m in range(4):
                    run(dense(((win, widx(19 + m), 8), yc_evac(m)), U, chunks, mix_ring))
                for m in range(2):
                    gate_bufs[m].old, gate_bufs[m].free = gate_bufs[m].free, None
                    gate_box[2, m]["b"] = gate_bufs[m]
                    run(dense(gate_job(2, m, None, gate_box[2, m]), U, chunks, mix_ring))
                merge(2, False, True)

            t_u = [(pe.sem, pe.count)]
            for m in range(KT):
                dep = [macc_tok[m, c] for c in range(len(chunks))]
                t1 = act(fn(uh[:, m, cols], macc[:, m, cols], ACT.Copy), dep, t_u)
                t2 = dve(tt(ul[:, m, cols], macc[:, m, cols], uh[:, m, cols], SUB), t1, t_u)
                U.t[m] = [t1, t2]
            t_m = [t1, t2]
            y_toks, wr = {}, {}
            t_y = [(pe.sem, pe.count), (dve.sem, dve.count), (act.sem, act.count)]

            def out_evac(m):
                def evac(c, c0, cn, ps, tok):
                    cs = slice(c0, c0 + cn)
                    if blk2:
                        t1 = dve(stt(h[:, m, cs], ps, 0.5, h[:, m, cs], MUL, ADD), tok)
                        wr[m, c] = t1
                        return t1
                    ta, tb_ = square_into_acc(m, ps, tok, cs, 0.5)
                    state["accw"] = tb_
                    t2 = act(fn(y_x[:, m, cs], ps, ACT.Identity, scale=pcol("mpost", l, m)), tok, t_y)
                    y_toks[m] = [t2]
                    wr["last"] = tb_
                    return [ta, t2]
                return evac

            jobs = [(("wout", ((2 if blk2 else l), m), 8), out_evac(m)) for m in range(KT)]
            dense_group(jobs[:3], U, chunks, ffn_ring, lambda: None)
            for j in jobs[3:]:
                run(dense(j, U, chunks, ffn_ring))
            state["u"] = [(pe.sem, pe.count)]
            if blk2:
                for m in range(KT):
                    state["last"], _ = prep(m, gain_next, [wr[m, 0], wr[m, 1]], cols)
                state["x"] = [(pe.sem, pe.count), t_m]
            else:
                rbt2, _ = rstd(1, wr["last"], False, 0.5)
                state["last"], reads = residual_and_prep(y_x, y_toks, rbt2, gain_next, cols)
                state["x"] = [reads, (pe.sem, pe.count), t_m]

        def g(name, l):
            return lambda m: pcol(name, l, m)

        def clear(n):
            for e in (pe, act, dve, pool, sp):
                del e.queue[n[e][0]:]
                e.count = n[e][1]
                e.waited = dict(n[e][2])
            for s, c in n["slots"].items():
                s.count = c

        def program():
            c1, ch1 = slice(X0, TW), [(X0, 512)]
            c2, ch2 = slice(0, TW), [(0, 264), (264, 264)]
            step = 0
            if W.order is not W.asked:
                W.split()
            for m in range(KT):
                state["last"], _ = prep(m, g("f1pre", 0), [t_x[m], t_par], c1)
            for l in range(2):
                if step >= limit:
                    break
                ffn(2 * l, l, 0, c1, ch1, False, g("mpre", l), g("f1post", l))
                step += 1
                if step >= limit:
                    break
                mix(l, False, ch1, c1, g("f2pre", l))
                step += 1
                if step >= limit:
                    break
                if l == 0:
                    ffn(1, l, 1, c1, ch1, False, g("f1pre", 1), g("f2post", 0))
                else:
                    t_meta = [sp.dma(slot(f"x{m}"), ld(h[:, m, 0:X0], T["metat"][m])) for m in range(KT)]
                    ffn(3, l, 1, c1, ch1, False, None, g("f2post", 1))
                step += 1
            if step < limit:
                y_toks, rbt = state["y"]
                for m in range(KT):
                    bq = temps.take()
                    t = dve(tt(bq.ap[:, c1], y_u[:, m, c1], rb[:, 1, c1], MUL), y_toks[m], rbt, bq.old)
                    t2 = pool(tt(h[:, m, c1], h[:, m, c1], bq.ap[:, c1], ADD), t)
                    bq.free = [t2]
                    state["u"] = state["u"] + [t]
                    state["last"], _ = prep(m, g("mpre", 2), [t2, t_meta[m]], c2)
                mix(2, True, ch2, c2, g("fpre", 2))
                step += 1
            if step < limit:
                ffn(4, 2, 0, c2, ch2, True, None, None)
                step += 1
            full = step < limit
            outs = []
            if full:
                rbt, _ = rstd(0, state["last"], True)
            else:
                everything = [(e.sem, e.count) for e in (pe, act, dve, pool)]
            for m in range(KT):
                bq = temps.take()
                if full:
                    t = dve(stt(bq.ap[:, X0:TW], h[:, m, X0:TW], pcol("final", 2, m), rb[:, 0, X0:TW], MUL, MUL), rbt, bq.old)
                else:
                    t = dve(cp(bq.ap[:, X0:TW], h[:, m, X0:TW]), everything, bq.old)
                tok = sp.dma(slot(f"o{m}"), ld(OUT[m], bq.ap[:, X0:TW]), t)
                bq.free = [tok]
                outs.append(tok)
            sp.final = outs

        snap = {e: (len(e.queue), e.count, dict(e.waited)) for e in (pe, act, dve, pool, sp)}
        snap["slots"] = {s: s.count for s in list(s_ld.values()) + raw_slots}
        st0 = {k: list(v) if isinstance(v, list) else v for k, v in state.items()}
        bufs0 = {id(b_): (b_, list(b_.free), b_.taken) for b_ in banks + temps.bufs}
        W.order = W.asked
        program()
        order = list(W.asked)
        clear(snap)
        for s in list(s_ld.values()):
            if s not in snap["slots"]:
                s.count = 0
        state.clear()
        state.update(st0)
        for b_, fr, tk in bufs0.values():
            b_.free, b_.taken = list(fr), tk
        temps.n = 2
        ffn_ring.n = mix_ring.n = pt_ring.n = 0
        unit_no[0] = 0
        U.t, G.t, OB.t = {}, {}, {}
        W = Weights(order)
        program()
        assert W.asked == order

        block = ctx.enter_context(nc.Block())

        def emit(e, q):
            for waits, make, inc in q.queue:
                for s, v in waits:
                    e.wait_ge(s, v)
                ins = make(e)
                if inc:
                    ins.then_inc(*inc)

        @block.tensor
        def _(e):
            emit(e, pe)

        @block.scalar
        def _(e):
            emit(e, act)

        @block.vector
        def _(e):
            emit(e, dve)

        @block.gpsimd
        def _(e):
            emit(e, pool)

        @block.sync
        def _(e):
            emit(e, sp)
            for s, v in flat(sp.final):
                e.wait_ge(s, v)


def program(nc, arrays, limit=99):
    T = {k: nc.dram_tensor(f"in_{k}", list(v.shape), F32, kind="ExternalInput").ap() for k, v in arrays.items()}
    out = nc.dram_tensor("out_t", [KT, P, 512], F32, kind="ExternalOutput").ap()
    cum = nc.dram_tensor("cum_d", [8, TW], F32, kind="Internal").ap()
    relv = nc.dram_tensor("relv_d", [8, P, 384], F32, kind="Internal").ap()
    build(nc, T, out, cum, relv, limit)


def kernel(**inputs):
    import numpy as _np
    import concourse.bacc as _bacc
    from concourse.bass_utils import run_bass_kernel_spmd as _run

    arrays = pack({k: _np.asarray(v) for k, v in inputs.items()})
    nc = _bacc.Bacc("TRN2", target_bir_lowering=False, num_devices=1)
    program(nc, arrays)
    r = _run(nc, [{f"in_{k}": v for k, v in arrays.items()}], core_ids=[0])
    o = r.results[0]["out_t"]
    return _np.ascontiguousarray(o.reshape(D, 512).T).reshape(1, 512, D)
```

```python
import math
from contextlib import ExitStack

import numpy as np

import concourse.bass as bass
from concourse import mybir

F32 = mybir.dt.float32
F32R = mybir.dt.float32r
ALU = mybir.AluOpType
ACT = mybir.ActivationFunctionType
AX = mybir.AxisListType

P = 128
D = 1024
KT = 8
FT = 22
TW = 528
X0 = 16
NEG = -1e30
AHEAD = 3
TICKS = {"A": (2, 2, 2, 2, 2, 2, 1, 1, 1, 1), "B": (2, 2, 1, 2, 1), "C": (4, 4, 4, 3, 3),
         "S": (2, 2, 2, 2, 3), "F": (1, 3, 3, 2, 2, 1, 2, 2, 1, 1)}
LOWEST = -3.0e38

def share(name, u):
    t = TICKS[name]
    return t[(5 * u[0] + u[1]) % len(t)]


PCOLS = {}
_n = 0
for _l in range(2):
    for _name, _w in (("f1pre", 8), ("f1post", 8), ("mpre", 8), ("mpost", 8), ("f2pre", 8), ("f2post", 8),
                      ("sink", 8), ("subg", 1), ("bgate", 24)):
        PCOLS[_name, _l] = _n
        _n += _w
for _name, _w in (("mpre", 8), ("fpre", 8), ("final", 8), ("sink", 8), ("foxb", 1), ("convw", 16), ("convb", 4),
                  ("br", 4), ("bi", 4), ("lam", 4)):
    PCOLS[_name, 2] = _n
    _n += _w
NPAR = _n


class Engine:

    def __init__(self, sem, always, serial=False):
        self.sem, self.always, self.serial = sem, always, serial
        self.queue, self.count, self.waited = [], 0, {}

    def __call__(self, make, *after, inc=False):
        waits = []
        if self.serial and self.count:
            after = (after, (self.sem, self.count))
        for sem, value in flat(after):
            if self.waited.get(id(sem), 0) < value:
                self.waited[id(sem)] = value
                waits.append((sem, value))
        inc = inc or self.always
        self.queue.append((waits, make, (self.sem, 1) if inc else None))
        if inc:
            self.count += 1
            return (self.sem, self.count)
        return None

    def dma(self, slot, make, *after):
        self(make, *after)
        if self.always:
            self.count -= 1
        waits, fn, _ = self.queue[-1]
        self.queue[-1] = (waits, fn, (slot.sem, 16))
        slot.count += 16
        return (slot.sem, slot.count)


class Slot:
    def __init__(self, sem):
        self.sem, self.count = sem, 0


class Buf:

    def __init__(self, ap):
        self.ap, self.free, self.taken = ap, [], 0


class Ring:
    clock = [0]

    def __init__(self, bufs):
        self.bufs = bufs

    def take(self):
        b = min((b for b in self.bufs if b.free is not None), key=lambda b: b.taken)
        self.clock[0] += 1
        b.taken, b.old, b.free = self.clock[0], b.free, None
        return b


def flat(x):
    for y in x:
        if y is None:
            continue
        if isinstance(y, tuple) and len(y) == 2 and isinstance(y[1], int):
            yield y
        else:
            yield from flat(y)


def consts():
    f = np.float32
    c = {}
    c["ident"] = np.eye(P, dtype=f)
    c["ones"] = np.ones((P, P), f)
    pos = np.arange(512, dtype=f)
    inv = (f(10000.0) ** (-np.arange(0, 64, 2, dtype=f) / f(64))).astype(f)
    ang = (pos[:, None] * inv[None, :]).astype(f)
    cos, sin = np.cos(ang).astype(f).T, np.sin(ang).astype(f).T
    c["cos"] = np.concatenate([cos] * 4, 0)
    c["sin"] = np.concatenate([sin, -sin] * 2, 0)
    col = np.arange(64)
    start = np.clip(col - 8, 0, 48)
    ok = (col[None, :] >= start[:, None]) & (col[None, :] < start[:, None] + 16)
    m = np.where(ok, 0.0, NEG).astype(f)
    c["mask_a"] = np.concatenate([m, m], 0)
    q, k = np.arange(P)[:, None], np.arange(3 * P)[None, :]
    c["mask_b"] = np.where(np.abs(q + P - k) <= 128, 0.0, NEG).astype(f)
    k2 = np.arange(2 * P)[None, :]
    dist = q + P - k2
    c["mask_s"] = np.where((dist >= 0) & (dist < 128), 0.0, NEG).astype(f)
    k1 = np.arange(P)[None, :]
    c["mask_t"] = np.where(k1 <= q, 0.0, NEG).astype(f)
    d = np.arange(128)
    scaled = np.log(np.maximum(d, 1).astype(f) / f(16)) / f(math.log(128 / 16))
    large = np.minimum(16 + (scaled * 16).astype(np.int32), 31)
    bucket = np.where(d < 16, d, large)
    oh = np.zeros((32, 384), f)
    oh[bucket, 255 - d] = 1.0
    c["onehot"] = oh
    return c


def tiles_t(w):
    k, n = w.shape
    return np.ascontiguousarray(w.reshape(k // P, P, n // P, P).transpose(2, 1, 0, 3))


def tiles_v(w):
    k, n = w.shape
    return np.ascontiguousarray(w.reshape(k // 256, 2, P, n).transpose(0, 2, 1, 3))


PAIRED = np.concatenate([np.arange(64) + 64 * h for t in range(4) for h in (t, t + 4)])


def pack(x):
    f = np.float32
    out = {}
    out["xt"] = np.ascontiguousarray(x["x"][0].T.reshape(KT, P, 512))
    out["metat"] = np.ascontiguousarray(x["meta_tokens_2"].T.reshape(KT, P, 16))
    out["gu"] = np.stack([tiles_t(a) for a in (x["ffn1_w_gu"][0], x["ffn2_w_gu"][0], x["ffn1_w_gu"][1],
                                               x["ffn2_w_gu"][1], x["w_ffn_in_2"][0])])
    out["dn"] = np.stack([tiles_t(a) for a in (x["ffn1_w_down"][0], x["ffn2_w_down"][0], x["ffn1_w_down"][1],
                                               x["ffn2_w_down"][1], x["w_ffn_out_2"][0])])
    ins, vs, brs = [], [], []
    for l in range(2):
        w = x["w_in"][l]
        ins.append(tiles_t(np.concatenate([w[:, 0:1024], w[:, 1536:2048][:, PAIRED], w[:, 2048:2304],
                                           w[:, 2304:3328], w[:, 3840:6912]], 1)))
        vs.append(np.stack([tiles_v(w[:, 1024:1536]), tiles_v(w[:, 3328:3840])]))
        b = x["w_branch"][l]
        brs.append(np.stack([tiles_t(b[0]), tiles_t(b[1][PAIRED]), tiles_t(b[2])]))
    out["win"], out["wv"] = np.stack(ins), np.stack(vs)
    w = x["w_in_2"][0]
    fl = np.concatenate([w[:, 2304:2312], np.zeros((D, 120), f)], 1)
    out["win2"] = tiles_t(np.concatenate([w[:, 0:512][:, PAIRED], w[:, 512:768], w[:, 768:1792], fl,
                                          w[:, 2312:3336], w[:, 3336:6408]], 1))
    out["wv2"] = tiles_v(w[:, 1792:2304])
    b = x["w_branch_2"][0]
    brs.append(np.stack([tiles_t(b[0][PAIRED]), tiles_t(b[1]), tiles_t(b[2])]))
    out["wbr"] = np.stack(brs)
    out["wout"] = np.stack([tiles_t(x["w_out"][0]), tiles_t(x["w_out"][1]), tiles_t(x["w_out_2"][0])])
    par = np.zeros((P, NPAR), f)

    def put(name, l, a):
        par[:, PCOLS[name, l]:PCOLS[name, l] + a.shape[1]] = a

    def cols(v):
        return v.reshape(-1, P).T

    for l in range(2):
        for name, src in (("f1pre", "ffn1_pre_g"), ("f1post", "ffn1_post_g"), ("mpre", "mix_pre_g"),
                          ("mpost", "mix_post_g"), ("f2pre", "ffn2_pre_g"), ("f2post", "ffn2_post_g"),
                          ("subg", "diff_subln_g")):
            put(name, l, cols(x[src][l]))
        put("sink", l, np.broadcast_to(x["sw_sink"][l], (P, 8)))
        put("bgate", l, cols(x["b_gate"][l].reshape(-1)))
    put("mpre", 2, cols(x["norm_mix_2"][0]))
    put("fpre", 2, cols(x["norm_ffn_2"][0]))
    put("final", 2, cols(x["norm_final_2"]))
    put("sink", 2, np.broadcast_to(x["swa_sinks_2"][0], (P, 8)))
    par[0:8, PCOLS["foxb", 2]] = x["fox_forget_bias_2"][0]
    put("convw", 2, cols(x["conv_w_2"][0].reshape(-1)))
    put("convb", 2, cols(x["conv_b_2"][0]))
    put("br", 2, cols(x["lru_b_r_2"][0]))
    put("bi", 2, cols(x["lru_b_i_2"][0]))
    put("lam", 2, cols(x["lru_lambda_2"][0]))
    out["par"] = par
    out["lamv"] = np.ascontiguousarray(np.broadcast_to(np.stack(
        [np.concatenate([x[f"diff_lambda_{a}"][l] for a in ("q1", "k1", "q2", "k2")]) for l in range(2)]
    ).reshape(1, 512), (P, 512)))
    rp = np.zeros((2, 8, 15, 64, P), f)
    rp[..., 48:79] = x["na_rpb"][:, :, :, None, :]
    out["rpb"] = rp
    lw = np.zeros((2, 4, P, P), f)
    for i, name in enumerate(("lru_w_r_2", "lru_w_i_2")):
        for b in range(8):
            o = 64 * (b % 2)
            lw[i, b // 2, o:o + 64, o:o + 64] = x[name][0][b]
    out["lruw"] = np.ascontiguousarray(lw.transpose(2, 0, 1, 3)).reshape(P, 1024)
    out["rel"] = np.ascontiguousarray(x["rel_bias_table_2"])
    for k, v in consts().items():
        out["c_" + k] = np.ascontiguousarray(v)
    return out


def build(nc, T, OUT, CUM, RELV, limit=99):
    ctx = ExitStack()
    Ring.clock[0] = 0
    with ctx:
        def sem(name):
            return ctx.enter_context(nc.semaphore(name))

        at = [16512]
        where = {}

        def area(name, size):
            where[name] = at[0]
            at[0] += size

        def sb(name, shape, dt, offset):
            return nc.alloc_sbuf_tensor_at(name, list(shape), dt, offset=offset)

        for name, size in (("h", 8 * TW * 4), ("uh", 8 * TW * 4), ("ul", 8 * TW * 4), ("raw", 3 * 4096),
                           ("split", 4 * 8192), ("tmp", 6 * TW * 4), ("acc", TW * 4), ("rb", 2 * TW * 4),
                           ("small", 1024), ("par", 1280), ("ident", 512), ("ones", 512), ("maskt", 512),
                           ("X", 44 * TW * 4)):
            area(name, size)
        h = sb("h", [P, 8, TW], F32, where["h"])
        uh = sb("uh", [P, 8, TW], F32R, where["uh"])
        ul = sb("ul", [P, 8, TW], F32R, where["ul"])
        y_u = sb("y_u", [P, 8, TW], F32, where["uh"])
        raw = sb("raw", [P, 3, 1024], F32, where["raw"])
        wh = sb("wh", [P, 4, 1024], F32R, where["split"])
        wl = sb("wl", [P, 4, 1024], F32R, where["split"] + 4 * 4096)
        tmpt = sb("tmpt", [P, 6, TW], F32, where["tmp"])
        acc = sb("acc", [P, TW], F32, where["acc"])
        rb = sb("rb", [P, 2, TW], F32, where["rb"])
        small = sb("small", [P, 256], F32, where["small"])
        par = sb("par", [P, NPAR + 64], F32, where["par"])
        ident = sb("ident", [P, P], F32, where["ident"])
        ones = sb("ones", [P, P], F32, where["ones"])
        maskt = sb("maskt", [P, P], F32, where["maskt"])
        X = where["X"]
        gh = sb("gh", [P, FT, TW], F32R, X)
        gl = sb("gl", [P, FT, TW], F32R, X + FT * TW * 4)
        stk = sb("stk", [P, 12, TW], F32R, X)
        y_x = sb("y_x", [P, 8, TW], F32, X)
        lru = sb("lru", [P, 20, 532], F32, X)
        XV = X + 12 * TW * 4
        V = sb("V", [P, 5, 512], F32, XV)
        PT = sb("PT", [P, 5, 512], F32, XV + 10240)
        XG = XV + 20480
        gates = sb("gates", [P, 2, TW], F32, XG)
        macc = sb("macc", [P, 8, TW], F32, XG + 2 * TW * 4)
        obh = sb("obh", [P, 4, TW], F32R, XG + 10 * TW * 4)
        obf = sb("obf", [P, 4, TW], F32, XG + 10 * TW * 4)
        obl = sb("obl", [P, 4, TW], F32R, XG + 14 * TW * 4)
        gate_v = sb("gate_v", [P, TW], F32, XV - 4 * X0)
        gate_p = sb("gate_p", [P, TW], F32, XV + 10240 - 4 * X0)
        stkf = sb("stkf", [P, 12, TW], F32, X)
        XT = XG + 18 * TW * 4
        tb = sb("tb", [P, 2, 896], F32, XT)
        maska = sb("maska", [P, 64], F32, XT + 7168)
        oblf = sb("oblf", [P, 4, TW], F32, XG + 14 * TW * 4)
        cos = sb("cos", [P, 512], F32, XT)
        sin = sb("sin", [P, 512], F32, XT + 2048)
        maskb = sb("maskb", [P, 384], F32, XT + 4096)
        sbias = sb("sbias", [P, 2, 256], F32, XT)
        masks = sb("masks", [P, 256], F32, XT + 2048)
        onehot = sb("onehot", [32, 384], F32, XT + 3072)
        relt = sb("relt", [32, 8], F32, XT + 4608)
        relv = sb("relv", [8, 384], F32, XT + 4640)
        cumb = sb("cumb", [P, 2, TW], F32, XT)
        ci = sb("ci", [P, 5, 8], F32, XT + 4224)
        cumt = sb("cumt", [8, TW], F32, XT + 4384)
        ptm = sb("ptm", [16, 16], F32, XT + 6496)
        assert NPAR * 4 + 256 <= 1280 and XT + 7168 + 256 <= X + 44 * TW * 4 <= nc.sbuf_usable_end

        PS = ctx.enter_context(nc.psum_tensor("PS", [P, 4096], F32))
        banks = [Buf(PS[:, 512 * i:512 * i + 512]) for i in range(8)]

        pe = Engine(sem("s_pe"), False)
        act = Engine(sem("s_act"), True)
        dve = Engine(sem("s_dve"), True)
        pool = Engine(sem("s_pool"), True, True)
        sp = Engine(None, False)
        raw_slots = [Slot(sem(f"s_raw{i}")) for i in range(3)]
        s_ld = {}

        def slot(name):
            if name not in s_ld:
                s_ld[name] = Slot(sem("s_" + name))
            return s_ld[name]

        def mm(out, lhsT, rhs, start, stop):
            return lambda e: e.matmul(out, lhsT, rhs, start=start, stop=stop, skip_group_check=True)

        def tr(out, in_, idn):
            return lambda e: e.transpose(out, in_, idn)

        def fn(out, in_, f, bias=None, scale=1.0, accum=None):
            kw = {} if bias is None else {"bias": bias}
            if accum is not None:
                kw["accum_out"] = accum
            return lambda e: e.activation(out, in_, f, scale=scale, **kw)

        def tt(out, a, b, op):
            return lambda e: e.tensor_tensor(out, a, b, op)

        def ts(out, a, s1, s2, op0, op1=None):
            if op1 is None:
                return lambda e: e.tensor_scalar(out, a, s1, None, op0)
            return lambda e: e.tensor_scalar(out, a, s1, s2, op0, op1)

        def stt(out, a, s, b, op0, op1):
            return lambda e: e.scalar_tensor_tensor(out, a, s, b, op0, op1)

        def rcp(out, a):
            return lambda e: e.reciprocal(out, a)

        def cp(out, a):
            return lambda e: e.tensor_copy(out, a)

        def ld(out, in_):
            return lambda e: e.dma_start(out, in_)

        MUL, ADD, SUB, MAX, MIN = ALU.mult, ALU.add, ALU.subtract, ALU.max, ALU.min

        def pcol(name, l, i=0):
            c = PCOLS[name, l] + i
            return par[:, c:c + 1]

        HB = NPAR
        EPSC, NLAM, SUBG, C8 = NPAR + 48, NPAR + 49, NPAR + 51, NPAR + 53
        NC8 = NPAR + 57
        eps = par[:, EPSC:EPSC + 1]

        t_par = sp.dma(slot("par"), ld(par[:, 0:NPAR], T["par"]))
        t_id = sp.dma(slot("id"), ld(ident[:, :], T["c_ident"]))
        t_on = sp.dma(slot("on"), ld(ones[:, :], T["c_ones"]))
        temps = Ring([Buf(tmpt[:, i, :]) for i in range(6)])
        t_eps = dve(lambda e: e.memset(eps, 1e-6))
        t_hb = []
        for l in range(2):
            c = PCOLS["bgate", l]
            t_hb.append(dve(ts(par[:, HB + 24 * l:HB + 24 * l + 24], par[:, c:c + 24], 0.5, None, MUL), t_par))
            lam_init = 0.8 - 0.6 * math.exp(-0.3 * l)
            t_sg = dve(ts(par[:, SUBG + l:SUBG + l + 1], pcol("subg", l), 1.0 - lam_init, None, MUL), t_par)
            t_hb.append(t_sg)
        decay = {}

        def lambdas():
            b, b2 = temps.take(), temps.take()
            t_lv = sp.dma(slot("lv"), ld(b.ap[:, 0:512], T["lamv"]), b.old)
            decay["mt"] = sp.dma(slot("mt"), ld(maskt[:, :], T["c_mask_t"]))
            lv = b.ap[:, 0:512].rearrange("p (l a k d) -> p l a k d", l=2, a=2, k=2)
            pr = b2.ap[:, 0:256].rearrange("p (l a d) -> p l a d", l=2, a=2)
            t1 = None
            for l in range(2):
                t1 = dve(tt(pr[:, l, :, :], lv[:, l, :, 0, :], lv[:, l, :, 1, :], MUL), t_lv, b2.old)
            t2 = dve(lambda e: e.tensor_reduce(small[:, 0:4].rearrange("p (l a) -> p l a", l=2), pr, AX.X, ADD), t1)
            t3 = act(fn(small[:, 4:8], small[:, 0:4], ACT.Exp), t2)
            sv = small[:, 4:8].rearrange("p (l a) -> p l a", l=2)
            t4 = dve(tt(par[:, NLAM:NLAM + 2], sv[:, :, 1], sv[:, :, 0], SUB), t3)
            for l in range(2):
                lam_init = 0.8 - 0.6 * math.exp(-0.3 * l)
                c = par[:, NLAM + l:NLAM + l + 1]
                decay["lam"] = dve(ts(c, c, -lam_init, None, ADD), t4)
            b.free, b2.free = [t1], [t2]

        flows = []

        def flow(gen):
            flows.append(gen)

        def point():
            for g_ in list(flows):
                if next(g_, "end") == "end":
                    flows.remove(g_)

        def settle():
            while flows:
                point()

        class Weights:

            def __init__(self, order):
                self.order, self.asked = order, []
                self.loaded, self.cut = {}, {}
                self.n_load = self.n_cut = self.n_done = 0
                self.raw_free = [None] * 3
                self.cut_free = [[] for _ in range(4)]

            def load(self):
                i = self.n_load
                if i >= len(self.order):
                    return
                name, idx, k0, kn = self.order[i]
                src = T[name][idx]
                n = kn * P
                if name in ("wv", "wv2"):
                    src = src.rearrange("p k n -> p (k n)")
                    n = 1024
                else:
                    src = src[:, k0:k0 + kn, :].rearrange("p k n -> p (k n)")
                self.loaded[i] = (sp.dma(raw_slots[i % 3], ld(raw[:, i % 3, 0:n], src), self.raw_free[i % 3]), n)
                self.n_load += 1

            def split(self):
                i = self.n_cut
                if i >= len(self.order):
                    return
                while self.n_load <= i:
                    self.load()
                t, n = self.loaded[i]
                r, a, b_ = raw[:, i % 3, 0:n], wh[:, i % 4, 0:n], wl[:, i % 4, 0:n]
                t_h = act(fn(a, r, ACT.Copy), t, self.cut_free[i % 4])
                t_l = dve(tt(b_, r, a, SUB), t_h, self.cut_free[i % 4])
                self.cut[i] = (t_h, t_l)
                self.raw_free[i % 3] = [t_h, t_l]
                self.n_cut += 1
                while self.n_load < i + 4 and self.n_load < len(self.order):
                    self.load()

            def get(self, spec):
                i = len(self.asked)
                self.asked.append(spec)
                if self.order and self.order is not self.asked:
                    assert self.order[i] == spec
                    while self.n_cut <= i:
                        self.split()
                    toks = self.cut[i]
                else:
                    toks = None
                return i, wh[:, i % 4, :], wl[:, i % 4, :], toks

            def ahead(self):
                if self.order is not self.asked and self.n_cut < min(len(self.order), self.n_done + 4):
                    self.split()

            def done(self, i, tok):
                self.cut_free[i % 4] = [tok]
                self.n_done = i + 1
                if self.order is not self.asked:
                    while self.n_cut <= i + AHEAD and self.n_cut < len(self.order):
                        self.split()

        W = Weights([])

        def jobs_of(name, idx, kt):
            return [(name, idx, k0, min(8, kt - k0)) for k0 in range(0, kt, 8)]

        def dense(job, X_, chunks, ring):
            (name, idx, kt), evac = job
            bb = [ring.take() for _ in chunks]
            specs = jobs_of(name, idx, kt)
            for s, spec in enumerate(specs):
                i, a, b_, toks = W.get(spec)
                n = 0
                for c, (c0, cn) in enumerate(chunks):
                    for k in range(spec[3]):
                        kk = spec[2] + k
                        first, last = kk == 0, kk == kt - 1
                        w1, w2 = a[:, k * P:k * P + P], b_[:, k * P:k * P + P]
                        o = bb[c].ap[:, 0:cn]
                        dep = [toks, X_.tok(kk, c)] + ([bb[c].old] if first else [])
                        pe(mm(o, w1, X_.hi(kk, c0, cn), first, False), dep)
                        pe(mm(o, w2, X_.hi(kk, c0, cn), False, False))
                        end = k == spec[3] - 1
                        t = pe(mm(o, w1, X_.lo(kk, c0, cn), False, last), inc=end)
                        n += 1
                        if n % 2 == 0 and not (end and c == len(chunks) - 1):
                            point()
                            yield
                    if s == len(specs) - 1:
                        bb[c].free = evac(c, c0, cn, bb[c].ap[:, 0:cn], t)
                        bb[c].free = list(flat([bb[c].free]))
                W.done(i, t)
                point()
                yield

        def dense_group(jobs, X_, chunks, ring, mid):
            bb = [[ring.take() for _ in chunks] for _ in jobs]
            got = [W.get(jobs_of(j[0][0], j[0][1], 8)[0]) for j in jobs]
            toks_end = {}
            for k in range(KT):
                for n, (i, a, b_, toks) in enumerate(got):
                    for c, (c0, cn) in enumerate(chunks):
                        o = bb[n][c].ap[:, 0:cn]
                        w1, w2 = a[:, k * P:k * P + P], b_[:, k * P:k * P + P]
                        pe(mm(o, w1, X_.hi(k, c0, cn), k == 0, False), toks, X_.tok(k, c), bb[n][c].old if k == 0 else None)
                        pe(mm(o, w2, X_.hi(k, c0, cn), False, False))
                        toks_end[n, c] = pe(mm(o, w1, X_.lo(k, c0, cn), False, k == 7), inc=k == 7)
            mid()
            W.ahead()
            for n, j in enumerate(jobs):
                for c, (c0, cn) in enumerate(chunks):
                    bb[n][c].free = list(flat([j[1](c, c0, cn, bb[n][c].ap[:, 0:cn], toks_end[n, c])]))
                W.done(got[n][0], toks_end[n, len(chunks) - 1])

        def run(gen):
            for _ in gen:
                pass

        class Operand:
            def __init__(self, hi, lo):
                self.h, self.l, self.t = hi, lo, {}

            def hi(self, k, c0, cn):
                return self.h[:, k, c0:c0 + cn]

            def lo(self, k, c0, cn):
                return self.l[:, k, c0:c0 + cn]

            def tok(self, k, c):
                return self.t.get((k, c), self.t.get(k))

        U = Operand(uh, ul)
        G = Operand(gh, gl)
        OB = Operand(obh, obl)

        ffn_ring = Ring([banks[i] for i in range(6)])
        ring_1 = Ring([banks[i] for i in range(2)])
        ring_2 = Ring([banks[i] for i in range(3)])

        state = {"acc": [], "rb0": [], "rb1": [], "rt": [], "u": [], "x": [], "hold": []}

        sq = {}

        def square_into_acc(m, src, tok, cols, scale=1.0, early=False):
            bq = temps.take()
            sq[m] = (bq, act(fn(bq.ap[:, cols], src, ACT.Square, scale=scale), tok, bq.old))
            t = sq[m][1]

            def rest():
                yield from ()
                if m in (1, 3, 5):
                    o, to = sq[m - 1]
                    dst = acc[:, cols] if m == 1 else bq.ap[:, cols]
                    t2 = dve(tt(dst, bq.ap[:, cols], o.ap[:, cols], ADD), t, to, state["acc"])
                    o.free = bq.free = [t2]
                    if m > 1:
                        t2 = pool(tt(acc[:, cols], acc[:, cols], bq.ap[:, cols], ADD), t2, sq["acc"])
                        bq.free = [t2]
                    sq["acc"] = t2
                elif m == 6:
                    sq["acc"] = pool(tt(acc[:, cols], acc[:, cols], bq.ap[:, cols], ADD), t, sq["acc"])
                    bq.free = [sq["acc"]]
                    if early:
                        yield
                        yield
                        first_sums(cols.start == 0)
            if m in (1, 3, 5, 6):
                flow(rest())
            return t

        def sums(blk2, a, src, dep):
            for j in range(0 if blk2 else 1, 5):
                q0 = 0 if j == 0 else X0 + P * (j - 1)
                c = 8 * a + j
                t = pe(mm(banks[6].ap[:, c:c + 1], src[:, q0:q0 + P], ones[:, 0:1], True, True), dep, t_on,
                       banks[6].free, inc=True)
            return t

        def first_sums(blk2):
            j0 = 0 if blk2 else 1
            t = sums(blk2, 0, acc, sq["acc"])
            state["acc"] = [t]
            sq["first"] = dve(cp(small[:, 16 + j0:21], banks[6].ap[:, j0:5]), t)

        def rstd(which, blk2, factor=1.0):
            tiles = [0, 1, 2, 3, 4] if blk2 else [1, 2, 3, 4]
            j0 = tiles[0]
            b6, b7 = banks[6], banks[7]
            settle()
            if "first" not in sq:
                first_sums(blk2)
            last, t7 = sq[7]
            sd, rt = small[:, 16 + j0:21], small[:, 8 + j0:13]
            t = sums(blk2, 1, last.ap, [t7, sq["first"]])
            last.free = [t]
            sq.clear()
            t = dve(tt(sd, sd, b6.ap[:, 8 + j0:13], ADD), t)
            t0 = t
            t = act(fn(sd, sd, ACT.Sqrt, bias=eps, scale=1.0 / D), t, t_eps)
            t_rt = dve(rcp(rt, sd), t, state["rt"])
            dg = temps.take()
            dt = []
            for j in tiles:
                n = 16 if j == 0 else P
                q0 = 0 if j == 0 else X0 + P * (j - 1)
                dt.append(dve(ts(dg.ap[0:n, q0:q0 + n], ident[0:n, 0:n], small[0:n, 8 + j:9 + j], None, MUL), t_rt,
                              dg.old, t_id))
            if which == 1:
                W.ahead()
            tb_ = pe(mm(b7.ap[:, :], ones[:, :], dg.ap[:, X0:TW], True, True), dt, b7.free, inc=True)
            tw = act(fn(rb[:, which, X0:TW], b7.ap[:, :], ACT.Copy, scale=factor), tb_, state[f"rb{which}"])
            b7.free = [tw]
            b6.free = [t0]
            out = [tw]
            if blk2:
                tb_ = pe(mm(b6.ap[:, 64:80], ones[0:16, :], dg.ap[0:16, 0:16], True, True), dt, t0, inc=True)
                tw = act(fn(rb[:, which, 0:X0], b6.ap[:, 64:80], ACT.Copy, scale=factor), tb_)
                b6.free = [tw]
                out.append(tw)
            dg.free = [tb_]
            return out, t_rt

        def prep(m, gain, tok, cols):
            point()
            g = gain(m)
            t1 = act(fn(uh[:, m, cols], h[:, m, cols], ACT.Identity, scale=g), tok, state["u"])
            square_into_acc(m, h[:, m, cols], tok, cols)
            u = list(flat([state["u"]]))

            def rest():
                yield from ()
                t2 = dve(stt(ul[:, m, cols], h[:, m, cols], g, uh[:, m, cols], MUL, SUB), t1, u)
                U.t[m] = [t1, t2]
            flow(rest())

        def residual_and_prep(y, y_toks, rb_toks, gain, cols, out_cols=None, more=None):
            reads, prod = [], []
            for m in range(KT + 1):
                if m < KT:
                    bq = temps.take()
                    t = dve(tt(bq.ap[:, cols], y[:, m, cols], rb[:, 1, cols], MUL), y_toks[m], rb_toks, bq.old)
                    t2 = pool(tt(h[:, m, cols], h[:, m, cols], bq.ap[:, cols], ADD), t)
                    bq.free = [t2]
                    reads.append(t)
                    prod.append((t, t2))
                if m > 0:
                    t, t2 = prod[m - 1]
                    if y is y_u:
                        state["u"] = state["u"] + [prod[min(m, KT - 1)][0], t]
                    prep(m - 1, gain, [t2, more[m - 1] if more else None], out_cols or cols)
            settle()
            state["rb1"] = reads
            return reads

        def ffn(w, l, which, cols, chunks, blk2, next_gain, post):
            z, rbt = {}, {}

            def mid():
                rbt["t"], t_rt = rstd(0, blk2)
                state["rt"] = []

            def gate_evac(f):
                def evac(c, c0, cn, ps, tok):
                    if c == 0:
                        z[f] = temps.take()
                        z[f].t = {}
                    a = z[f].ap[:, c0:c0 + cn]
                    t1 = dve(tt(a, ps, rb[:, 0, c0:c0 + cn], MUL), tok, rbt["t"], z[f].old)
                    t2 = act(fn(a, a, ACT.Silu), t1)
                    z[f].t[c] = pool(tt(a, a, rb[:, 0, c0:c0 + cn], MUL), t2)
                    state["rb0"] = [z[f].t[c]]
                    return t1
                return evac

            def up_evac(f):
                def evac(c, c0, cn, ps, tok):
                    bq = temps.take()
                    a = bq.ap[:, c0:c0 + cn]
                    t1 = dve(tt(a, ps, z[f].ap[:, c0:c0 + cn], MUL), tok, z[f].t[c], bq.old)
                    t2 = act(fn(gh[:, f, c0:c0 + cn], a, ACT.Copy), t1, state["x"])
                    t3 = dve(tt(gl[:, f, c0:c0 + cn], a, gh[:, f, c0:c0 + cn], SUB), t2, state["x"])
                    bq.free = [t2, t3]
                    if c == len(chunks) - 1:
                        z[f].free = [t1]
                    G.t[f, c] = [t2, t3]
                    return t1
                return evac

            jobs = []
            for f in range(FT):
                jobs.append((("gu", (w, f), 8), gate_evac(f)))
                jobs.append((("gu", (w, FT + f), 8), up_evac(f)))
            G.t = {}
            dense_group(jobs[:3], U, chunks, ffn_ring, mid)
            if w == 0:
                lambdas()
                flow(lambda_of_decay())
            for j in jobs[3:]:
                run(dense(j, U, chunks, ffn_ring))
            state["u"] = [(pe.sem, pe.count)]
            y_toks = {}
            wr = {}

            def down_evac(m):
                def evac(c, c0, cn, ps, tok):
                    cs = slice(c0, c0 + cn)
                    if post is None:
                        t1 = dve(tt(h[:, m, cs], ps, h[:, m, cs], ADD), tok)
                        wr[m, c] = t1
                        if c == len(chunks) - 1:
                            square_into_acc(m, h[:, m, cols], [wr[m, i] for i in range(len(chunks))], cols, 1.0, True)
                        return t1
                    ta = square_into_acc(m, ps, tok, cs, 1.0, True)
                    t2 = act(fn(y_u[:, m, cs], ps, ACT.Identity, scale=post(m)), tok, state["u"])
                    y_toks[m] = [t2]
                    return [ta, t2]
                return evac

            for m in range(KT):
                run(dense((("dn", (w, m), FT), down_evac(m)), G, chunks, ffn_ring))
            state["x"] = [(pe.sem, pe.count)]
            if post is None:
                return
            rbt2, _ = rstd(1, blk2, 0.5)
            if next_gain is None:
                state["y"] = (y_toks, rbt2)
                return
            residual_and_prep(y_u, y_toks, rbt2, next_gain, cols)

        pt_ring = Ring([banks[6], banks[7]])

        class Filler:

            def __init__(self, stacks):
                self.items, self.done, self.active, self.pair = [], set(), None, 0
                self.settled, self.stacks = set(), stacks

            def add(self, name, gen, pair=0):
                self.items.append((name, gen, pair))

            def tick(self, n=1):
                while n > 0:
                    if self.active is None:
                        ok = [i for i in self.items if i[2] <= self.pair + 1]
                        if not ok:
                            return
                        self.active = ok[0]
                        self.items.remove(ok[0])
                    if next(self.active[1], "end") == "end":
                        self.done.add(self.active[0])
                        self.active = None
                    else:
                        n -= 1

            def finish(self, name=None):
                if name is None:
                    self.pair = 99
                while (self.items or self.active) and (name is None or name not in self.done):
                    self.tick()

            def need(self, pair, name, kinds="qk"):
                self.pair = pair
                if pair and name not in self.settled:
                    self.finish(name)
                    while not all((name[0], kind, pair) in self.stacks for kind in kinds):
                        point()
                    self.settled.add(name)

        def ktok(i):
            return (0, 16) if i == 0 else (X0 + P * (i - 1), P)

        def attention(units, smax, pv, filler, ticks, lag=2, end=True):

            def stage2(u, info):
                x, j, kts = u
                e_buf, e_tok = info
                qn = 16 if j == 0 else P
                big = [i for i in kts if i > 0]
                frees = []
                shared = 0 in kts and j > 0 and 4 not in big
                if 0 in kts:
                    bk = (pt_ring if shared else ring_2).take()
                    z0 = 384 if shared else 0
                    t = pe(tr(bk.ap[0:16, z0:z0 + qn], e_buf.ap[0:qn, 0:16], ident[0:qn, 0:qn]), e_tok, bk.old, t_id,
                           inc=True)
                    dst = ptm[:, :] if j == 0 else PT[0:16, 0, P * (j - 1):P * j]
                    frees.append(t)
                    if not shared:
                        t2 = act(fn(dst, bk.ap[0:16, z0:z0 + qn], ACT.Copy), t, state["pt", j])
                        bk.free = [t2]
                        pt_tok[x, j, 0] = t2
                if big and j > 0:
                    if not shared:
                        bk = pt_ring.take()
                    for i in big:
                        k0, kn = ktok(i)
                        t = pe(tr(bk.ap[:, P * (i - 1):P * i], e_buf.ap[:, k0:k0 + kn], ident[:, :]), e_tok, bk.old,
                               t_id, inc=i == big[-1])
                    if shared:
                        t3 = act(fn(dst, bk.ap[0:16, z0:z0 + qn], ACT.Copy), t, state["pt", j])
                        pt_tok[x, j, 0] = t3
                    a, z_ = big[0], big[-1] + 1
                    t2 = act(fn(PT[:, a:z_, P * (j - 1):P * j],
                                bk.ap[:, P * (a - 1):P * (z_ - 1)].rearrange("p (i q) -> p i q", q=P), ACT.Copy), t,
                             state["pt", j])
                    bk.free = [t2]
                    pt_tok[x, j, 1] = t2
                    frees.append(t)
                e_buf.free = frees

            settle()
            filler.pair = 0
            pt_tok = {}
            attention.pt_tok = pt_tok
            ends, info, meta = {}, {}, None
            for n in range(len(units) + lag + 2):
                if n < len(units):
                    ends[n] = smax(units[n])
                if 0 <= n - 1 < len(units):
                    info[n - 1] = ends.pop(n - 1)()
                point()
                filler.tick(ticks(units[n]) if n < len(units) else 1)
                if 0 <= n - lag < len(units):
                    stage2(units[n - lag], info.pop(n - lag))
                if 0 <= n - lag - 2:
                    if units[n - lag - 2][1] == 0:
                        meta = units[n - lag - 2]
                    else:
                        pv(*units[n - lag - 2])
                        if meta:
                            pv(*meta)
                        meta = None
            if end:
                settle()

        def scores(q, kh, kl, j, keys, bank, deps):
            q0 = 0 if j == 0 else X0 + P * (j - 1)
            k0, k1 = keys
            if bank is None:
                off = 2048 + 496
                segs = [(a, b_) for a, b_ in ((k0, min(k1, X0)), (max(k0, X0), k1)) if a < b_]
                olds = [banks[4].free, banks[5].free]
            else:
                off = 512 * bank - k0
                segs = [(k0, k1)]
                olds = banks[bank].free
            for a, b_ in segs:
                o = PS[:, off + a:off + b_]
                pe(mm(o, q[:, q0:q0 + P], kh[:, a:b_], True, False), deps, olds)
                t = pe(mm(o, q[:, q0:q0 + P], kl[:, a:b_], False, True), inc=True)
            return PS[:, off + k0:off + k1], t

        def s_free(bank, toks):
            for i in (4, 5) if bank is None else (bank,):
                banks[i].free = toks

        unit_no = [0]

        def sm(i):
            c = 64 + (unit_no[0] % 8) * 16 + i
            return small[:, c:c + 1]

        def expsum(dst, e, neg, after, sink, rows=P):
            r = slice(0, rows)
            l_, d_, es = sm(2)[r], sm(3)[r], sm(4)[r]
            t1 = act(fn(dst, e, ACT.Exp, bias=neg[r], accum=l_), after)
            t2 = None
            if sink is not None:
                t2 = act(fn(es, sink[r], ACT.Exp, bias=neg[r]), after)

            def end():
                dep = [t1]
                if sink is not None:
                    dep = [dve(tt(l_, l_, es, ADD), t1, t2)]
                return d_, dve(rcp(d_, l_), dep)
            return t1, end

        def build_stack(src, tok, slots, kind, cols, free):
            toks = {0: [], 1: []}
            own = [slice(64 * hh, 64 * hh + 64) for hh in range(2)]
            oth = [own[1], own[0]]
            for hh in range(2):
                a = slots[hh] if kind == "q" else slots[hh][0]
                toks[hh].append(act(fn(stk[own[hh], a, cols], src[own[hh], cols], ACT.Copy), tok, free))
            if kind != "q":
                for hh in range(2):
                    a = slots[hh][0]
                    toks[hh].append(act(fn(stk[oth[hh], a, cols], src[own[hh], cols], ACT.Copy), tok, free))
            yield
            for hh in range(2):
                t1 = toks[hh][0]
                if kind == "q":
                    s = slots[hh]
                    toks[hh].append(dve(tt(stk[oth[hh], s, cols], src[own[hh], cols], stk[own[hh], s, cols], SUB), t1,
                                        free))
                else:
                    a, b_ = slots[hh]
                    for r in (own[hh], oth[hh]):
                        toks[hh].append(dve(tt(stk[r, b_, cols], src[own[hh], cols], stk[own[hh], a, cols], SUB), t1,
                                            free))
            return toks

        def mix(l, blk2, chunks, cols, gain_next):
            xt = state["x"]
            rbt = {}
            branch_mats = "wbr"
            win = "win2" if blk2 else "win"
            tiles = [0, 1, 2, 3, 4] if blk2 else [1, 2, 3, 4]

            def widx(i):
                return (i,) if blk2 else (l, i)

            def mid():
                rbt["t"], rbt["rt"] = rstd(0, blk2)
                state["rt"] = []

            stack_tok = {}
            stack_free = {}

            def to_stack(key, slots, kind, rope, free):
                st = {}

                def to_stack_rest(bq, b2, ts_):
                    yield
                    if rope:
                        xs = slice(X0, TW)
                        r = []
                        for qd in range(4):
                            a = slice(32 * qd, 32 * qd + 32)
                            o = slice(32 * (qd ^ 1), 32 * (qd ^ 1) + 32)
                            eng = dve if qd == 0 else pool
                            r.append(eng(tt(b2.ap[o, xs], bq.ap[a, xs], sin[a, :], MUL), ts_, b2.old, rbt["tab"]))
                        yield
                        t2 = dve(tt(bq.ap[:, xs], bq.ap[:, xs], cos[:, :], MUL), r, rbt["tab"])
                        t3 = dve(tt(bq.ap[:, xs], bq.ap[:, xs], b2.ap[:, xs], ADD), t2, r)
                        b2.free = [t3]
                        ts_ = [t3]
                        yield
                    toks = yield from build_stack(bq.ap, ts_, slots, kind, cols, free())
                    bq.free = [toks[0], toks[1]]
                    stack_tok[key] = toks

                def evac(c, c0, cn, ps, tok):
                    cs = slice(c0, c0 + cn)
                    if c == 0:
                        st["b"] = temps.take()
                        st["t"] = []
                    bq = st["b"]
                    if kind == "q":
                        t1 = dve(stt(bq.ap[:, cs], ps, 0.125, rb[:, 0, cs], MUL, MUL), tok, rbt["t"], bq.old)
                    else:
                        t1 = dve(tt(bq.ap[:, cs], ps, rb[:, 0, cs], MUL), tok, rbt["t"], bq.old)
                    st["t"].append(t1)
                    state["rb0"] = [t1]
                    if c == len(chunks) - 1:
                        b2 = temps.take() if rope else None
                        flow(to_stack_rest(bq, b2, list(st["t"])))
                    return t1
                return evac

            def gate_job(n, m, dst, tok_box):
                base = 23 if blk2 else 22

                def evac(c, c0, cn, ps, tok):
                    cs = slice(c0, c0 + cn)
                    if c == 0 and callable(dst):
                        tok_box["b"] = dst()
                    bq = tok_box["b"]
                    t1 = dve(tt(bq.ap[:, cs], ps, rb[:, 0, cs], MUL), tok, rbt["t"], bq.old)
                    state["rb0"] = [t1]
                    bias = 0.0 if blk2 else par[:, HB + 24 * l + 8 * n + m:HB + 24 * l + 8 * n + m + 1]
                    tok_box[c] = act(fn(bq.ap[:, cs], bq.ap[:, cs], ACT.Tanh, bias=bias, scale=0.5), t1, t_hb)
                    return t1
                return ((win, widx(base + 8 * n + m), 8), evac)

            mix_ring = ring_2 if blk2 else ring_1
            gate_bufs = [Buf(gates[:, i, :]) for i in range(2)]
            if not blk2:
                gate_bufs += [Buf(gate_v[:, :]), Buf(gate_p[:, :])] + [Buf(stkf[:, i, :]) for i in range(8, 12)]
            macc_tok = {}

            def merge(n, first):
                for m in range(KT):
                    box = gate_box[n, m]
                    if "b" not in box:
                        run(dense(gate_job(n, m, temps.take, box), U, chunks, ffn_ring))

                    def evac(c, c0, cn, ps, tok, m=m, box=box):
                        cs = slice(c0, c0 + cn)
                        dst = macc[:, m, cs]
                        g = box["b"].ap[:, cs]
                        if first:
                            t1 = dve(stt(dst, g, 1.0, ps, ADD, MUL), tok, box[c])
                            t2 = t1
                        else:
                            t1 = dve(stt(g, g, 1.0, ps, ADD, MUL), tok, box[c])
                            t2 = pool(tt(dst, dst, g, ADD), t1, macc_tok[m, c])
                        macc_tok[m, c] = t2
                        if c == len(chunks) - 1:
                            box["b"].free = [macc_tok[m, i] for i in range(len(chunks))]
                        return t1
                    run(dense(((branch_mats, ((2 if blk2 else l), n, m), 4), evac), OB, chunks, ffn_ring))
                    yield
                state["ob"] = [(pe.sem, pe.count)]

            gate_box = {(n, m): {} for n in range(3) for m in range(KT)}
            state["ob"] = xt
            t_zero = []
            if blk2:
                t_zero = [dve(lambda e: e.memset(V[:, 0, :], 0.0), xt), dve(lambda e: e.memset(PT[:, 0, :], 0.0), xt)]
            for j in range(5):
                state["pt", j] = list(xt) + t_zero
            state["v"] = list(xt) + t_zero
            for b_ in gate_bufs:
                b_.free = list(xt)

            def gate_early(n, m, where):
                def gen():
                    where.old, where.free = where.free, None
                    gate_box[n, m]["b"] = where
                    yield from dense(gate_job(n, m, None, gate_box[n, m]), U, chunks, mix_ring)
                return gen()

            def macc_buf(m):
                b_ = Buf(macc[:, m, :])
                b_.free = list(xt)
                return b_

            def gate_fill(filler, n, wheres, skip=0, pair=0):
                for m, w_ in enumerate(wheres):
                    if m >= skip:
                        filler.add(("gate", n, m), gate_early(n, m, w_), pair)

            def values(vname, vidx):
                vb = [banks[3], banks[4], banks[5], banks[6], banks[7]][:len(tiles)]
                olds = [b_.free for b_ in vb]
                for kc in range(4):
                    i, a, b_, toks = W.get((vname, vidx + (kc,), 0, 8))
                    for n, j in enumerate(tiles):
                        q0 = 0 if j == 0 else X0 + P * (j - 1)
                        for k2 in range(2):
                            kk = 2 * kc + k2
                            w1, w2 = a[:, 512 * k2:512 * k2 + 512], b_[:, 512 * k2:512 * k2 + 512]
                            o = vb[n].ap
                            u1, u2 = uh[:, kk, q0:q0 + P], ul[:, kk, q0:q0 + P]
                            pe(mm(o, u1, w1, kk == 0, False), toks, U.tok(kk, 0), olds[n] if kk == 0 else None)
                            pe(mm(o, u1, w2, False, False))
                            if k2 == 0 and n % 2:
                                point()
                            t = pe(mm(o, u2, w1, False, kk == 7), inc=k2 == 1)
                        if kc == 3:
                            r = slice(0, 16 if j == 0 else P)
                            t2 = act(fn(V[r, j, :], o[r, :], ACT.Copy, scale=small[r, 8 + j:9 + j]), t, rbt["rt"],
                                     state["v"])
                            vb[n].free = [t2]
                            v_tok.append(t2)
                    W.done(i, t)

            v_tok = []

            def values_from_t(job_idx):
                st = {}

                def rest(bq):
                    yield
                    yield
                    yield
                    bk = pt_ring.take()
                    for j in tiles[-4:]:
                        t = pe(tr(bk.ap[:, P * (j - 1):P * j], bq.ap[:, X0 + P * (j - 1):X0 + P * j], ident[:, :]),
                               st["t"], bk.old, t_id, inc=True)
                    t2 = act(fn(V[:, 1:5, 0:P], bk.ap[:, :].rearrange("p (j d) -> p j d", d=P), ACT.Copy), t,
                             state["v"])
                    bk.free = [t2]
                    v_tok.append(t2)
                    if blk2:
                        bk = pt_ring.take()
                        t = pe(tr(bk.ap[0:16, 0:P], bq.ap[:, 0:16], ident[:, :]), st["t"], bk.old, inc=True)
                        t2 = act(fn(V[0:16, 0, 0:P], bk.ap[0:16, 0:P], ACT.Copy), t, state["v"])
                        bk.free = [t2]
                        v_tok.append(t2)
                    bq.free = [t]

                def evac(c, c0, cn, ps, tok):
                    if c == 0:
                        st["b"] = temps.take()
                        st["t"] = []
                    bq = st["b"]
                    cs = slice(c0, c0 + cn)
                    t1 = dve(tt(bq.ap[:, cs], ps, rb[:, 0, cs], MUL), tok, rbt["t"], bq.old)
                    state["rb0"] = [t1]
                    st["t"].append(t1)
                    if c == len(chunks) - 1:
                        flow(rest(bq))
                    return t1
                return ((win, widx(job_idx), 8), evac)

            def pv_plain(pairs, vcol, o_ring):
                cur = {}

                def pv(x, j, kts):
                    t_, par_ = pairs(x)
                    rows = slice(64 * par_, 64 * par_ + 64)
                    vc = vcol(x)
                    deps = [attention.pt_tok.get((x, j, a)) for a in range(2)]
                    if j == 0:
                        bk = ring_2.take()
                        t = pe(mm(bk.ap[:, 0:16], V[0:16, 0, vc], ptm[:, :], True, True), deps, v_tok, bk.old, inc=True)
                        cs = slice(0, 16)
                        src = bk.ap[rows, 0:16]
                    else:
                        if j == 1:
                            cur["b"] = o_ring.take()
                        bk = cur["b"]
                        c = slice(P * (j - 1), P * j)
                        for i in kts:
                            t = pe(mm(bk.ap[:, c], V[:, i, vc], PT[:, i, c], i == kts[0], i == kts[-1]),
                                   deps, v_tok, bk.old, inc=i == kts[-1])
                        cs = slice(X0, TW)
                        src = bk.ap[rows, :]
                    state["pt", j] = [t]
                    state["v"] = [t]
                    if j in (0, 4):
                        def out():
                            t1 = act(fn(obh[rows, t_, cs], src, ACT.Copy), t, state["ob"])
                            if j == 4:
                                yield
                            t2 = dve(tt(obl[rows, t_, cs], src, obh[rows, t_, cs], SUB), t1, state["ob"])
                            bk.free = [t1, t2]
                            OB.t.setdefault(t_, []).extend([t1, t2])
                        flow(out())
                        point()
                return pv

            filler = Filler(stack_tok)

            def free_of(key):
                return lambda: stack_free.get(key, list(xt))

            def pair_slots(p):
                s = 6 * (p % 2)
                return [s, s + 3], [(s + 1, s + 2), (s + 4, s + 5)]

            def proj_pair(tag, p, qi, ki, rope):
                qs, ks = pair_slots(p)
                return [((win, widx(qi + p), 8), to_stack((tag, "q", p), qs, "q", rope, free_of(p % 2))),
                        ((win, widx(ki + p), 8), to_stack((tag, "k", p), ks, "k", rope, free_of(p % 2)))]

            def add_proj(filler, tag, p, qi, ki, rope):
                for n, j in enumerate(proj_pair(tag, p, qi, ki, rope)):
                    filler.add((tag, p, n), dense(j, U, chunks, mix_ring), p)

            def done_unit(p, tok):
                stack_free[p % 2] = [tok]

            first_group = {"done": False}

            def start(jobs):
                if not first_group["done"]:
                    dense_group(jobs, U, chunks, ffn_ring, mid)
                    first_group["done"] = True
                else:
                    for j in jobs:
                        run(dense(j, U, chunks, ffn_ring))

            if not blk2:
                tabs = [sp.dma(slot("tab1"), ld(cos[:, :], T["c_cos"]), xt),
                        sp.dma(slot("tab2"), ld(sin[:, :], T["c_sin"]), xt),
                        sp.dma(slot("tab3"), ld(maskb[:, :], T["c_mask_b"]), xt)]
                rbt["tab"] = tabs

                jobs = proj_pair("C", 0, 14, 18, True)
                first_gate = macc_buf(0)
                first_gate.old, first_gate.free = first_gate.free, None
                gate_box[0, 0]["b"] = first_gate
                jobs.append(gate_job(2, 0, None, gate_box[0, 0]))
                gate_box[2, 0] = gate_box[0, 0]
                gate_box[0, 0] = {}
                start(jobs)
                values("wv", (l, 1))
                for p in range(1, 4):
                    add_proj(filler, "C", p, 14, 18, True)
                gate_fill(filler, 2, [macc_buf(m) for m in range(KT)], 1)
                c_bank = [0]
                e_ring = Ring(gate_bufs[:4])

                def smax_c(u):
                    x, j, kts = u
                    filler.need(x, ("C", x, 1))
                    qs, ks = pair_slots(x)
                    res = []
                    for s in range(2):
                        bank = (2, 4, 5)[c_bank[0] % 3]
                        c_bank[0] += 1
                        S, ts_ = scores(stk[:, qs[s], :], stk[:, ks[s][0], :], stk[:, ks[s][1], :], j, (X0, TW), bank,
                                        [stack_tok["C", "q", x][s], stack_tok["C", "k", x][s]])
                        eb = (e_ring if s else temps).take()
                        e = eb.ap[:, X0:TW]
                        ng = sm(1)
                        t1 = dve(lambda en, ng=ng, S=S: en.tensor_reduce(ng, S, AX.X, MAX, negate=True), ts_)
                        te, end = expsum(e, S, ng, [t1, ts_, eb.old], None)
                        s_free(bank, [te])
                        res.append((eb, e, end))
                        unit_no[0] += 1
                    done_unit(x, ts_)

                    def fin():
                        (e0b, e0, end0), (e1b, e1, end1) = res
                        d0, ta = end0()
                        d1, tb_ = end1()
                        t5 = act(fn(e0, e0, ACT.Copy, scale=d0), ta)
                        t6 = dve(ts(d1, d1, par[:, NLAM + l:NLAM + l + 1], None, MUL), tb_, decay["lam"])
                        t7 = dve(stt(e0, e1, d1, e0, MUL, ADD), t5, t6)
                        e1b.free = [t7]
                        return e0b, t7
                    return fin

                c_state = {}
                o_bank = banks[3]

                def pv_c(x, j, kts):
                    c = slice(P * (j - 1), P * j)
                    for i in kts:
                        t = pe(mm(o_bank.ap[:, c], V[:, i, P * x:P * x + P], PT[:, i, c], i == 1, i == 4),
                               attention.pt_tok[x, j, 1], v_tok, o_bank.free, inc=i == 4)
                    state["pt", j] = [t]
                    state["v"] = [t]
                    if j < 4:
                        return
                    t1 = act(fn(obf[:, x, X0:TW], o_bank.ap, ACT.Copy), t, state["ob"])
                    t2 = act(fn(oblf[:, x, X0:TW], o_bank.ap, ACT.Square), t, state["ob"])
                    o_bank.free = [t1, t2]

                    def squares():
                        yield
                        yield
                        bk = pt_ring.take()
                        for i in range(4):
                            t = pe(mm(bk.ap[:, i:i + 1], oblf[:, x, X0 + P * i:X0 + P * i + P], ones[:, 0:1], True, True),
                                   t2, bk.old, inc=True)
                        t3 = act(fn(small[:, 32 + 4 * x:36 + 4 * x], bk.ap[:, 0:4], ACT.Copy), t)
                        bk.free = [t3]
                        c_state[x] = [t1, t3]
                    flow(squares())

                units = [(x, j, [1, 2, 3, 4]) for x in range(4) for j in range(1, 5)]
                OB.t = {}
                attention(units, smax_c, pv_c, filler, lambda u: share("C", u), 2, False)
                filler.finish()
                all_free = [(pe.sem, pe.count)]
                v_tok.clear()
                kslots = [(4, 5), (6, 7)]
                next_jobs = [((win, widx(12), 8), to_stack(("B", "k"), kslots, "k", True, lambda: all_free)),
                             ((win, widx(8), 8), to_stack(("B", "q", 0), [0, 1], "q", True, lambda: all_free)),
                             values_from_t(13)]
                for b_ in gate_bufs[4:]:
                    b_.free = all_free

                def diagonals(x):
                    dg = temps.take()
                    return dg, [dve(ts(dg.ap[:, X0 + P * j:X0 + P * j + P], ident[:, :], small[:, 32 + 4 * x + j:33 + 4 * x + j],
                                       None, MUL), tb_, dg.old) for j in range(4)]

                def scaled(x, bk, t):
                    tp = temps.take()
                    t1 = dve(stt(tp.ap[:, X0:TW], obf[:, x, X0:TW], par[:, SUBG + l:SUBG + l + 1], bk.ap, MUL, MUL), t,
                             tp.old, c_state[x])
                    bk.free = [t1]
                    t2 = act(fn(obh[:, x, X0:TW], tp.ap[:, X0:TW], ACT.Copy), t1)
                    yield
                    t3 = dve(tt(obl[:, x, X0:TW], tp.ap[:, X0:TW], obh[:, x, X0:TW], SUB), t2, state["ob"])
                    tp.free = [t2, t3]
                    OB.t[x] = [t2, t3]

                start([next_jobs.pop(0)])
                while len(c_state) < 4:
                    point()
                ta = act(fn(small[:, 32:48], small[:, 32:48], ACT.Sqrt, bias=eps, scale=1.0 / P),
                         [c_state[x] for x in range(4)])
                tb_ = dve(rcp(small[:, 32:48], small[:, 32:48]), ta)
                dg, dt = diagonals(0)
                for x in range(4):
                    if next_jobs:
                        start([next_jobs.pop(0)])
                    else:
                        run(gate_early(1, x - 2, gate_bufs[x - 2]))
                    bk = pt_ring.take()
                    t = pe(mm(bk.ap[:, :], ones[:, :], dg.ap[:, X0:TW], True, True), dt, bk.old, inc=True)
                    dg.free = [t]
                    if x < 3:
                        dg, dt = diagonals(x + 1)
                    flow(scaled(x, bk, t))
                    point()
                point()
                settle()
                run(merge(2, True))

                bq_free = {1: all_free}
                for p in range(1, 4):
                    filler.add(("B", p, 0), dense(((win, widx(8 + p), 8), to_stack(("B", "q", p), [2 * (p % 2), 2 * (p % 2) + 1],
                               "q", True, (lambda p=p: bq_free.get(p % 2, all_free)))), U, chunks, mix_ring), p)
                gate_fill(filler, 1, gate_bufs, 2)

                def smax_b(u):
                    x, j, kts = u
                    p, hh = x // 2, x % 2
                    filler.need(p, ("B", p, 0), "q")
                    head = p + 4 * hh
                    bank = 4 + unit_no[0] % 2
                    k0, k1 = X0 + P * (kts[0] - 1), X0 + P * kts[-1]
                    S, ts_ = scores(stk[:, 2 * (p % 2) + hh, :], stk[:, kslots[hh][0], :], stk[:, kslots[hh][1], :], j,
                                    (k0, k1), bank, [stack_tok["B", "q", p][hh], stack_tok["B", "k"][hh]])
                    bq_free[p % 2] = [ts_]
                    eb = temps.take()
                    e = eb.ap[:, k0:k1]
                    mx, ng = sm(0), sm(1)
                    off = P if j == 1 else 0
                    mk = maskb[:, off:off + (k1 - k0)]
                    sink = pcol("sink", l, head)
                    t1 = dve(lambda en: en.tensor_tensor_reduce(e, S, mk, 1.0, sink, ADD, MAX, mx), ts_, eb.old, tabs)
                    s_free(bank, [t1])
                    t2 = dve(ts(ng, mx, -1.0, None, MUL), t1)
                    te, end = expsum(e, e, ng, t2, sink)
                    unit_no[0] += 1

                    def fin():
                        d_, t4 = end()
                        return eb, dve(ts(e, e, d_, None, MUL), t4)
                    return fin

                units = [(x, j, [i for i in (j - 1, j, j + 1) if 1 <= i <= 4]) for x in range(8) for j in range(1, 5)]
                OB.t = {}
                attention(units, smax_b, pv_plain(lambda x: (x // 2, x % 2), lambda x: slice(0, P),
                                                  Ring([banks[3], banks[2]])), filler, lambda u: share("B", u), 3)
                filler.finish()

                all_free = [(pe.sem, pe.count)]
                t_a = [(pool.sem, pool.count), (dve.sem, dve.count)]
                t_ma = sp.dma(slot("tab0"), ld(maska[:, :], T["c_mask_a"]), t_a)
                tb_bufs = [Buf(tb[:, i, :]) for i in range(2)]
                for b_ in tb_bufs:
                    b_.free = list(t_a)
                tb_tok = {}

                def load_tb(x):
                    if x >= 8:
                        return
                    bf = tb_bufs[x % 2]
                    th = T["rpb"].tensor
                    base = (l * 8 + x) * 15 * 64 * P + 63
                    dst = bf.ap.rearrange("p (r c) -> p r c", c=64)
                    ta = pool.dma(slot(f"tb{x % 2}"), ld(dst[0:64], bass.AP(th, base + 64 * P, [[127, 64], [64 * P, 14], [1, 64]])),
                                  bf.free)
                    tb2 = pool.dma(slot(f"tb{x % 2}"), ld(dst[64:128], bass.AP(th, base, [[127, 64], [64 * P, 14], [1, 64]])),
                                   bf.free)
                    m_ = maska[:, :].unsqueeze(1).to_broadcast([P, 14, 64])
                    tb_tok[x] = pool(tt(dst, dst, m_, ADD), ta, tb2, t_ma)

                v_tok.clear()
                stack_free[0] = all_free
                start(proj_pair("A", 0, 0, 4, False))
                values("wv", (l, 0))
                run(merge(1, False))
                load_tb(0)
                load_tb(1)
                stack_free[1] = [all_free, [b_.free for b_ in gate_bufs[4:]]]
                for p in range(1, 4):
                    add_proj(filler, "A", p, 0, 4, False)
                gate_fill(filler, 0, gate_bufs[:4], 0, 2)

                def smax_a(u):
                    x, j, kts = u
                    p, hh = x // 2, x % 2
                    filler.need(p, ("A", p, 1))
                    qs, ks = pair_slots(p)
                    bank = 4 + unit_no[0] % 2
                    S, ts_ = scores(stk[:, qs[hh], :], stk[:, ks[hh][0], :], stk[:, ks[hh][1], :], j, (X0, TW), bank,
                                    [stack_tok["A", "q", p][hh], stack_tok["A", "k", p][hh]])
                    done_unit(p, ts_)
                    eb = temps.take()
                    e = eb.ap[:, X0:TW]
                    mx, ng = sm(0), sm(1)
                    off = (6 - 2 * (j - 1)) * 64
                    tbl = tb_bufs[x % 2].ap[:, off:off + 512]
                    t1 = dve(lambda en: en.tensor_tensor_reduce(e, S, tbl, 1.0, LOWEST, ADD, MAX, mx), ts_, eb.old,
                             tb_tok[x])
                    s_free(bank, [t1])
                    t2 = dve(ts(ng, mx, -1.0, None, MUL), t1)
                    te, end = expsum(e, e, ng, t2, None)
                    unit_no[0] += 1
                    if j == 4:
                        tb_bufs[x % 2].free = [t1]
                        load_tb(x + 2)

                    def fin():
                        d_, t4 = end()
                        return eb, dve(ts(e, e, d_, None, MUL), t4)
                    return fin

                units = [(x, j, [1, 2, 3, 4]) for x in range(8) for j in range(1, 5)]
                OB.t = {}
                attention(units, smax_a, pv_plain(lambda x: (x // 2, x % 2), lambda x: slice(P * (x // 2), P * (x // 2) + P),
                                                  Ring([banks[3], banks[2]])), filler, lambda u: share("A", u), 3)
                filler.finish()
                run(merge(0, False))

            if blk2:
                t_oh = sp.dma(slot("tab0"), ld(onehot[:, :], T["c_onehot"]), xt)
                t_re = sp.dma(slot("tab1"), ld(relt[:, :], T["rel"]), xt)
                t_ms = sp.dma(slot("tab2"), ld(masks[:, :], T["c_mask_s"]), xt)
                bk = banks[7]
                t = pe(mm(bk.ap[0:8, 0:384], relt[:, :], onehot[:, :], True, True), t_oh, t_re, bk.free, inc=True)
                t = act(fn(relv[:, :], bk.ap[0:8, 0:384], ACT.Copy), t)
                bk.free = [t]
                t_rv = pool.dma(slot("rv"), ld(RELV, relv[:, :].unsqueeze(1).to_broadcast([8, P, 384])), t)
                sbufs = [Buf(sbias[:, i, :]) for i in range(2)]
                for b_ in sbufs:
                    b_.free = list(xt)
                sb_tok = {}

                def head_of(x):
                    return x // 2 + 4 * (x % 2)

                def load_sb(x):
                    if x >= 8:
                        return
                    bf = sbufs[x % 2]
                    src = bass.AP(RELV.tensor, head_of(x) * P * 384 + 127, [[383, P], [1, 256]])
                    t = pool.dma(slot(f"tb{x % 2}"), ld(bf.ap, src), bf.free, t_rv)
                    sb_tok[x] = pool(tt(bf.ap, bf.ap, masks[:, :], ADD), t, t_ms)

                load_sb(0)
                load_sb(1)
                kslots = [(8, 9), (10, 11)]
                jobs = [((win, widx(4), 8), to_stack(("S", "k"), kslots, "k", False, lambda: xt)),
                        ((win, widx(0), 8), to_stack(("S", "q", 0), [0, 1], "q", False, lambda: xt)),
                        values_from_t(5)]
                start(jobs)
                sq_free = {}
                for p in range(1, 4):
                    filler.add(("S", p, 0), dense(((win, widx(p), 8), to_stack(("S", "q", p), [2 * (p % 2), 2 * (p % 2) + 1],
                               "q", False, (lambda p=p: sq_free.get(p % 2, xt)))), U, chunks, mix_ring), p)
                run(gate_early(0, 0, macc_buf(0)))
                gate_fill(filler, 0, [macc_buf(m) for m in range(KT)], 1)

                def smax_s(u):
                    x, j, kts = u
                    p, hh = x // 2, x % 2
                    filler.need(p, ("S", p, 0), "q")
                    head = head_of(x)
                    rows = 16 if j == 0 else P
                    bank = 4 + unit_no[0] % 2
                    k0, k1 = ktok(kts[0])[0], sum(ktok(kts[-1]))
                    S, ts_ = scores(stk[:, 2 * (p % 2) + hh, :], stk[:, kslots[hh][0], :], stk[:, kslots[hh][1], :], j,
                                    (k0, k1), bank, [stack_tok["S", "q", p][hh], stack_tok["S", "k"][hh]])
                    sq_free[p % 2] = [ts_]
                    eb = temps.take()
                    r = slice(0, rows)
                    e = eb.ap[r, k0:k1]
                    mx, ng = sm(0), sm(1)
                    off = P if j == 0 else (256 - (k1 - k0))
                    bias = sbufs[x % 2].ap[r, off:off + (k1 - k0)]
                    sink = pcol("sink", 2, head)
                    t1 = dve(lambda en: en.tensor_tensor_reduce(e, S[r], bias, 1.0, sink[r], ADD, MAX, mx[r]), ts_, eb.old,
                             sb_tok[x])
                    s_free(bank, [t1])
                    t2 = dve(ts(ng[r], mx[r], -1.0, None, MUL), t1)
                    te, end = expsum(e, e, ng, t2, sink, rows)
                    unit_no[0] += 1
                    if j == 4:
                        sbufs[x % 2].free = [t1]
                        load_sb(x + 2)

                    def fin():
                        d_, t4 = end()
                        return eb, dve(ts(e, e, d_, None, MUL), t4)
                    return fin

                units = [(x, j, [i for i in (j - 1, j) if i >= 0]) for x in range(8) for j in range(5)]
                OB.t = {}
                attention(units, smax_s, pv_plain(lambda x: (x // 2, x % 2), lambda x: slice(0, P), Ring([banks[3]])),
                          filler, lambda u: share("S", u), 3)
                filler.finish()
                merge_s = merge(0, True)

                all_free = [(pe.sem, pe.count)]
                stack_free[0] = stack_free[1] = all_free
                v_tok.clear()
                t_prev = [(dve.sem, dve.count), (pool.sem, pool.count)]
                fx = {}

                def fl_evac(c, c0, cn, ps, tok):
                    cs = slice(c0, c0 + cn)
                    if c == 0:
                        fx["z"] = temps.take()
                    z_ = fx["z"].ap[0:8, cs]
                    t1 = dve(tt(z_, ps[0:8, :], rb[0:8, 0, cs], MUL), tok, rbt["t"], fx["z"].old)
                    state["rb0"] = [t1]
                    fx[c] = t1
                    return t1

                start([((win, widx(14), 8), fl_evac)])
                cbufs = [Buf(cumb[:, i, :]) for i in range(2)]
                cb_tok = {}

                def load_cb(x):
                    if x >= 8:
                        return
                    src = bass.AP(CUM.tensor, x * TW, [[0, P], [1, TW]])
                    cb_tok[x] = pool.dma(slot(f"tb{x % 2}"), ld(cbufs[x % 2].ap, src), cbufs[x % 2].free, t_cs[0])

                t_cs = []

                def cumulate(td_):
                    z_ = fx["z"].ap[0:8, :]
                    ta_, tb2, tc_ = cumb[0:8, 0, :], cumb[0:8, 1, :], acc[0:8, :]
                    t = dve(ts(z_, z_, par[0:8, PCOLS["foxb", 2]:PCOLS["foxb", 2] + 1], None, ADD), fx[0], fx[1])
                    t = yield from log_sigmoid(z_, ta_, tb2, tc_, td_.ap[0:8, :], z_, [t, t_prev, td_.old, state["acc"]])
                    t = dve(lambda e: e.memset(ta_, 1.0), t)
                    t_cum = dve(lambda e: e.tensor_tensor_scan(cumt[:, :], ta_, z_, 0.0, MUL, ADD), t, t_prev)
                    state["acc"] = [state["acc"], t_cum]
                    for b_ in [fx["z"], td_] + cbufs:
                        b_.free = [t_cum]
                    t_cs.append(pool.dma(slot("rv"), ld(CUM, cumt[:, :]), t_cum))
                    load_cb(0)
                    load_cb(1)
                    fx["cum"] = t_cum

                start(proj_pair("F", 0, 6, 10, False))
                flow(cumulate(temps.take()))
                values("wv2", ())
                run(merge_s)
                settle()
                bk = pt_ring.take()
                for j in range(5):
                    q0 = 0 if j == 0 else X0 + P * (j - 1)
                    t = pe(tr(bk.ap[:, 8 * j:8 * j + 8], cumt[:, q0:q0 + P], ident[0:8, 0:8]), fx["cum"], bk.old, inc=True)
                fx["ci"] = act(fn(ci[:, :, :], bk.ap[:, 0:40].rearrange("p (j h) -> p j h", h=8), ACT.Copy), t, t_prev)
                bk.free = [fx["ci"]]
                for p in range(1, 4):
                    add_proj(filler, "F", p, 6, 10, False)
                gate_fill(filler, 1, gate_bufs, 0, 3)

                def smax_f(u):
                    x, j, kts = u
                    p, hh = x // 2, x % 2
                    filler.need(p, ("F", p, 1))
                    qs, ks = pair_slots(p)
                    rows = 16 if j == 0 else P
                    bank = None if j == 4 else 4 + unit_no[0] % 2
                    r = slice(0, rows)
                    k1 = sum(ktok(j))
                    S, ts_ = scores(stk[:, qs[hh], :], stk[:, ks[hh][0], :], stk[:, ks[hh][1], :], j, (0, k1), bank,
                                    [stack_tok["F", "q", p][hh], stack_tok["F", "k", p][hh]])
                    done_unit(p, ts_)
                    eb = temps.take()
                    e = eb.ap[r, 0:k1]
                    ng = sm(1)
                    t1 = dve(stt(e, S[r], ci[r, j, x:x + 1], cbufs[x % 2].ap[r, 0:k1], ADD, SUB), ts_, eb.old, fx["ci"],
                             cb_tok[x])
                    s_free(bank, [t1])
                    dg_ = eb.ap[r, k1 - rows:k1]
                    t2 = dve(tt(dg_, dg_, maskt[r, 0:rows], ADD), t1, decay["mt"])
                    t3 = dve(lambda en: en.tensor_reduce(ng[r], e, AX.X, MAX, negate=True), t2)
                    te, end = expsum(e, e, ng, t3, None, rows)
                    unit_no[0] += 1
                    if j == 4:
                        cbufs[x % 2].free = [t1]
                        load_cb(x + 2)

                    def fin():
                        d_, t4 = end()
                        return eb, act(fn(e, e, ACT.Copy, scale=d_), t4)
                    return fin

                units = [(x, j, list(range(j + 1))) for x in range(8) for j in range(5)]
                OB.t = {}
                attention(units, smax_f, pv_plain(lambda x: (x // 2, x % 2), lambda x: slice(P * (x // 2), P * (x // 2) + P),
                                                 Ring([banks[3]])), filler, lambda u: share("F", u), 3)
                filler.finish()
                t_att = [(pe.sem, pe.count), (act.sem, act.count), (dve.sem, dve.count)]
                lwt = lru[:, 18:20, 0:512]
                t_lw = sp.dma(slot("tab3"), ld(lwt, T["lruw"].rearrange("p (a n) -> p a n", a=2)), t_att)
                lr = {}
                t_z = dve(lambda e: e.memset(lru[:, 0:4, 0:3], 0.0), t_att)

                def xc_evac(m):
                    def conv():
                        cw = PCOLS["convw", 2]
                        cv = lru[:, 4 + m, 0:TW]
                        t = dve(ts(cv, lru[:, m, 0:TW], par[:, cw + m:cw + m + 1], pcol("convb", 2, m), MUL, ADD), t_z,
                                lr["x", m, 0], lr["x", m, 1])
                        for i in range(1, 4):
                            if i % 2:
                                yield
                            t = dve(stt(cv, lru[:, m, i:i + TW], par[:, cw + 4 * i + m:cw + 4 * i + m + 1], cv, MUL, ADD), t)
                        lr["c", m] = t

                    def evac(c, c0, cn, ps, tok):
                        t1 = dve(tt(lru[:, m, 3 + c0:3 + c0 + cn], ps, rb[:, 0, c0:c0 + cn], MUL), tok, rbt["t"], t_att)
                        state["rb0"] = [t1]
                        lr["x", m, c] = t1
                        if c == 1:
                            flow(conv())
                        return t1
                    return evac

                for m in range(4):
                    run(dense(((win, widx(15 + m), 8), xc_evac(m)), U, chunks, ffn_ring))
                merge_f = merge(1, False)
                next(merge_f)
                settle()
                next(merge_f)
                for m in range(4):
                    for a, (name, row) in enumerate((("br", 8), ("bi", 12))):
                        for c, (c0, cn) in enumerate(chunks):
                            bk = ffn_ring.take()
                            t = pe(mm(bk.ap[:, 0:cn], lwt[:, a, P * m:P * m + P], lru[:, 4 + m, c0:c0 + cn], True, True),
                                   t_lw, lr["c", m], bk.old, inc=True)
                            t1 = act(fn(lru[:, row + m, c0:c0 + cn], bk.ap[:, 0:cn], ACT.Sigmoid,
                                        bias=pcol(name, 2, m)), t, t_att)
                            bk.free = [t1]
                            lr[name, m] = t1
                    lr["pg", m] = t
                next(merge_f)
                gb = [temps.take() for _ in range(4)]
                for m in range(4):
                    lr["t", m] = act(fn(lru[:, m, 0:TW], lru[:, 8 + m, 0:TW], ACT.Tanh, scale=par[:, NC8 + m:NC8 + m + 1]),
                                     lr["br", m], decay["t"], lr["c", m])
                    lr["g", m] = pool(tt(lru[:, 12 + m, 0:TW], lru[:, 12 + m, 0:TW], lru[:, 4 + m, 0:TW], MUL), lr["bi", m])
                for m in range(4):
                    r_ = lru[:, 8 + m, 0:TW]
                    lr["a", m] = act(fn(r_, r_, ACT.Exp, scale=par[:, C8 + m:C8 + m + 1]), lr["t", m])
                next(merge_f)
                for m in range(4):
                    r_, f_ = lru[:, 8 + m, 0:TW], lru[:, m, 0:TW]
                    t3 = dve(tt(gb[m].ap, r_, r_, MUL), lr["a", m], gb[m].old)
                    lr["s", m] = dve(stt(gb[m].ap, gb[m].ap, 1.0, f_, ADD, MUL), t3)
                    if m % 2:
                        next(merge_f)
                for m in range(4):
                    lr["s", m] = act(fn(gb[m].ap, gb[m].ap, ACT.Sqrt), lr["s", m])
                next(merge_f)
                for m in range(4):
                    t7 = dve(tt(gb[m].ap, gb[m].ap, lru[:, 12 + m, 0:TW], MUL), lr["s", m], lr["g", m])
                    t8 = dve(lambda e, m=m: e.tensor_tensor_scan(lru[:, 12 + m, 0:TW], lru[:, 8 + m, 0:TW], gb[m].ap, 0.0,
                                                                 MUL, ADD), t7)
                    gb[m].free = [t8]
                    lr["h", m] = t8
                    if m == 1:
                        next(merge_f)
                run(merge_f)
                OB.t = {}

                def yc_evac(m):
                    y_ = lru[:, 4 + m, 0:TW]

                    def rest(b1):
                        yield
                        t2 = dve(tt(b1.ap, y_, y_, MUL), lr["yt", m, 0], lr["yt", m, 1], b1.old)
                        t3 = dve(ts(b1.ap, b1.ap, 0.044715, 1.0, MUL, ADD), t2)
                        t4 = dve(tt(b1.ap, b1.ap, y_, MUL), t3)
                        t5 = act(fn(b1.ap, b1.ap, ACT.Tanh, scale=math.sqrt(2.0 / math.pi)), t4)
                        yield
                        t6 = dve(stt(b1.ap, b1.ap, 1.0, y_, ADD, MUL), t5)
                        t7 = dve(stt(b1.ap, b1.ap, 0.5, lru[:, 12 + m, 0:TW], MUL, MUL), t6, lr["h", m])
                        t8 = act(fn(obh[:, m, :], b1.ap, ACT.Copy), t7, state["ob"])
                        yield
                        t9 = dve(tt(obl[:, m, :], b1.ap, obh[:, m, :], SUB), t8, state["ob"])
                        b1.free = [t8, t9]
                        OB.t[m] = [t8, t9]

                    def evac(c, c0, cn, ps, tok):
                        t1 = dve(tt(y_[:, c0:c0 + cn], ps, rb[:, 0, c0:c0 + cn], MUL), tok, rbt["t"], lr["g", m],
                                 lr["pg", m])
                        state["rb0"] = [t1]
                        lr["yt", m, c] = t1
                        if c == 1:
                            flow(rest(temps.take()))
                        return t1
                    return evac

                for m in range(4):
                    run(dense(((win, widx(19 + m), 8), yc_evac(m)), U, chunks, ffn_ring))
                for m in range(2):
                    run(gate_early(2, m, gate_bufs[m]))
                settle()
                run(merge(2, False))

            t_u = [(pe.sem, pe.count)]
            for m in range(KT):
                dep = [macc_tok[m, c] for c in range(len(chunks))]
                t1 = act(fn(uh[:, m, cols], macc[:, m, cols], ACT.Copy), dep, t_u)
                t2 = dve(tt(ul[:, m, cols], macc[:, m, cols], uh[:, m, cols], SUB), t1, t_u)
                U.t[m] = [t1, t2]
            t_m = [t1, t2]
            y_toks, wr = {}, {}
            t_y = [(pe.sem, pe.count), (dve.sem, dve.count), (act.sem, act.count)]

            def out_evac(m):
                def evac(c, c0, cn, ps, tok):
                    cs = slice(c0, c0 + cn)
                    if blk2:
                        t1 = dve(stt(h[:, m, cs], ps, 0.5, h[:, m, cs], MUL, ADD), tok)
                        wr[m, c] = t1
                        return t1
                    ta = square_into_acc(m, ps, tok, cs, 0.5, True)
                    t2 = act(fn(y_x[:, m, cs], ps, ACT.Identity, scale=pcol("mpost", l, m)), tok, t_y)
                    y_toks[m] = [t2]
                    return [ta, t2]
                return evac

            jobs = [(("wout", ((2 if blk2 else l), m), 8), out_evac(m)) for m in range(KT)]
            dense_group(jobs[:3], U, chunks, ffn_ring, lambda: None)
            for j in jobs[3:]:
                run(dense(j, U, chunks, ffn_ring))
            state["u"] = [(pe.sem, pe.count)]
            if blk2:
                for m in range(KT):
                    prep(m, gain_next, [wr[m, 0], wr[m, 1]], cols)
                settle()
                state["x"] = [(pe.sem, pe.count), t_m]
            else:
                rbt2, _ = rstd(1, False, 0.5)
                reads = residual_and_prep(y_x, y_toks, rbt2, gain_next, cols)
                state["x"] = [reads, (pe.sem, pe.count), t_m]

        def log_sigmoid(x_ap, a_ap, b_ap, s_ap, p_ap, out_ap, tok):
            t = dve(ts(a_ap, x_ap, -1.0, None, MUL), tok)
            t = dve(tt(a_ap, a_ap, x_ap, MAX), t)
            t = act(fn(a_ap, a_ap, ACT.Exp, scale=-1.0), t)
            yield
            t = dve(ts(b_ap, a_ap, 2.0, None, ADD), t)
            t = dve(rcp(b_ap, b_ap), t)
            yield
            t = dve(tt(s_ap, a_ap, b_ap, MUL), t)
            t = dve(tt(b_ap, s_ap, s_ap, MUL), t)
            t = dve(ts(p_ap, b_ap, 1.0 / 17, 1.0 / 15, MUL, ADD), t)
            yield
            for k in (13, 11, 9, 7, 5, 3, 1):
                t = dve(tt(p_ap, p_ap, b_ap, MUL), t)
                t = dve(ts(p_ap, p_ap, 1.0 / k, None, ADD), t)
                if k % 4 == 1:
                    yield
            t = dve(tt(p_ap, p_ap, s_ap, MUL), t)
            t = dve(ts(a_ap, x_ap, 0.0, None, MIN), t)
            return dve(stt(out_ap, p_ap, -2.0, a_ap, MUL, ADD), t)

        def lambda_of_decay():
            t = yield from log_sigmoid(par[:, PCOLS["lam", 2]:PCOLS["lam", 2] + 4], small[:, 208:212], small[:, 212:216],
                                       small[:, 216:220], small[:, 220:224], small[:, 224:228], t_par)
            dve(ts(par[:, C8:C8 + 4], small[:, 224:228], 8.0, None, MUL), t)
            decay["t"] = dve(ts(par[:, NC8:NC8 + 4], small[:, 224:228], -8.0, None, MUL), t)

        def g(name, l):
            return lambda m: pcol(name, l, m)

        def clear(n):
            for e in (pe, act, dve, pool, sp):
                del e.queue[n[e][0]:]
                e.count = n[e][1]
                e.waited = dict(n[e][2])
            for s, c in n["slots"].items():
                s.count = c

        def program():
            c1, ch1 = slice(X0, TW), [(X0, 512)]
            c2, ch2 = slice(0, TW), [(0, 264), (264, 264)]
            step = 0
            t_x = []
            for m in range(KT):
                t_x.append(sp.dma(slot(f"x{m}"), ld(h[:, m, X0:TW], T["xt"][m])))
                if m in (0, 2, 4) and W.order is not W.asked:
                    W.load()
            if W.order is not W.asked:
                W.split()
            for m in range(KT):
                prep(m, g("f1pre", 0), [t_x[m], t_par], c1)
                if m in (0, 2) and W.order is not W.asked:
                    W.split()
            settle()
            for l in range(2):
                if step >= limit:
                    break
                ffn(2 * l, l, 0, c1, ch1, False, g("mpre", l), g("f1post", l))
                step += 1
                if step >= limit:
                    break
                mix(l, False, ch1, c1, g("f2pre", l))
                step += 1
                if step >= limit:
                    break
                if l == 0:
                    ffn(1, l, 1, c1, ch1, False, g("f1pre", 1), g("f2post", 0))
                else:
                    t_meta = [sp.dma(slot(f"x{m}"), ld(h[:, m, 0:X0], T["metat"][m])) for m in range(KT)]
                    ffn(3, l, 1, c1, ch1, False, None, g("f2post", 1))
                step += 1
            if step < limit:
                y_toks, rbt = state["y"]
                residual_and_prep(y_u, y_toks, rbt, g("mpre", 2), c1, c2, t_meta)
                mix(2, True, ch2, c2, g("fpre", 2))
                step += 1
            if step < limit:
                ffn(4, 2, 0, c2, ch2, True, None, None)
                step += 1
            full = step < limit
            outs = []
            if full:
                rbt, _ = rstd(0, True)
            else:
                everything = [(e.sem, e.count) for e in (pe, act, dve, pool)]
            for m in range(KT):
                bq = temps.take()
                if full:
                    t = dve(stt(bq.ap[:, X0:TW], h[:, m, X0:TW], pcol("final", 2, m), rb[:, 0, X0:TW], MUL, MUL), rbt, bq.old)
                else:
                    t = dve(cp(bq.ap[:, X0:TW], h[:, m, X0:TW]), everything, bq.old)
                tok = sp.dma(slot(f"o{m}"), ld(OUT[m], bq.ap[:, X0:TW]), t)
                bq.free = [tok]
                outs.append(tok)
            sp.final = outs

        snap = {e: (len(e.queue), e.count, dict(e.waited)) for e in (pe, act, dve, pool, sp)}
        snap["slots"] = {s: s.count for s in list(s_ld.values()) + raw_slots}
        st0 = {k: list(v) if isinstance(v, list) else v for k, v in state.items()}
        bufs0 = {id(b_): (b_, list(b_.free), b_.taken) for b_ in banks + temps.bufs}
        clock0 = Ring.clock[0]
        W.order = W.asked
        program()
        order = list(W.asked)
        clear(snap)
        for s in list(s_ld.values()):
            if s not in snap["slots"]:
                s.count = 0
        state.clear()
        state.update(st0)
        for b_, fr, tk in bufs0.values():
            b_.free, b_.taken = list(fr), tk
        Ring.clock[0] = clock0
        unit_no[0] = 0
        U.t, G.t, OB.t = {}, {}, {}
        W = Weights(order)
        program()
        assert W.asked == order

        block = ctx.enter_context(nc.Block())

        def emit(e, q):
            for waits, make, inc in q.queue:
                for s, v in waits:
                    e.wait_ge(s, v)
                ins = make(e)
                if inc:
                    ins.then_inc(*inc)

        @block.tensor
        def _(e):
            emit(e, pe)

        @block.scalar
        def _(e):
            emit(e, act)

        @block.vector
        def _(e):
            emit(e, dve)

        @block.gpsimd
        def _(e):
            emit(e, pool)

        @block.sync
        def _(e):
            emit(e, sp)
            for s, v in flat(sp.final):
                e.wait_ge(s, v)


def program(nc, arrays, limit=99):
    T = {k: nc.dram_tensor(f"in_{k}", list(v.shape), F32, kind="ExternalInput").ap() for k, v in arrays.items()}
    out = nc.dram_tensor("out_t", [KT, P, 512], F32, kind="ExternalOutput").ap()
    cum = nc.dram_tensor("cum_d", [8, TW], F32, kind="Internal").ap()
    relv = nc.dram_tensor("relv_d", [8, P, 384], F32, kind="Internal").ap()
    build(nc, T, out, cum, relv, limit)


def kernel(**inputs):
    import numpy as _np
    import concourse.bacc as _bacc
    from concourse.bass_utils import run_bass_kernel_spmd as _run

    arrays = pack({k: _np.asarray(v) for k, v in inputs.items()})
    nc = _bacc.Bacc("TRN2", target_bir_lowering=False, num_devices=1)
    program(nc, arrays)
    r = _run(nc, [{f"in_{k}": v for k, v in arrays.items()}], core_ids=[0])
    o = r.results[0]["out_t"]
    return _np.ascontiguousarray(o.reshape(D, 512).T).reshape(1, 512, D)
```
